# Optimizing a Trainium2 kernel written in Bass

```python
import jax, jax.numpy as jnp
from jax import lax
import numpy as np

D_MODEL = 2048
BATCH = 1
SEQ = 256
DEPTH = 2

CHUNK = 64
Q_BLOCK = 128
SB_HEADS = 8
SB_HEAD_DIM = 128
SB_WIDTH = SB_HEADS * SB_HEAD_DIM
MLA_HEADS = 8
MLA_NOPE = 128
MLA_ROPE = 64
MLA_V = 128
MLA_Q_LORA = 768
MLA_KV_LORA = 512
ROPE_THETA = 10000.0
D_FF = 5632
CONV_WIDTH = 3
EPS = 1e-6
IN_SPLITS = [SB_WIDTH, SB_WIDTH, SB_WIDTH, MLA_Q_LORA, MLA_KV_LORA, MLA_ROPE, D_MODEL, D_MODEL]
IN_COLS = int(sum(IN_SPLITS))

kernel_name = "hybrid_stickbreak_mla_convffn"

def rms_norm(x, g):
    xf = x.astype(jnp.float32)
    y = xf * lax.rsqrt(jnp.mean(xf * xf, axis=-1, keepdims=True) + EPS)
    return (y * g.astype(jnp.float32)).astype(x.dtype)

def rope_tables(seq, dim, dtype):
    inv = 1.0 / (ROPE_THETA ** (jnp.arange(0, dim, 2, dtype=jnp.float32) / dim))
    ang = jnp.arange(seq, dtype=jnp.float32)[:, None] * inv[None, :]
    return jnp.cos(ang).astype(dtype), jnp.sin(ang).astype(dtype)

def apply_rope(x, cos, sin):
    x1, x2 = jnp.split(x, 2, axis=-1)
    return jnp.concatenate([x1 * cos - x2 * sin, x1 * sin + x2 * cos], axis=-1)

def to_heads(t, n_heads):
    b, s, _ = t.shape
    return t.reshape(b, s, n_heads, -1).transpose(0, 2, 1, 3)

def from_heads(t):
    b, h, s, d = t.shape
    return t.transpose(0, 2, 1, 3).reshape(b, s, h * d)

def stick_breaking_attention(q, k, v):
    s_len = q.shape[2]
    scale = q.shape[-1] ** -0.5
    outs = []
    for blk in range(s_len // Q_BLOCK):
        q0 = blk * Q_BLOCK
        end = q0 + Q_BLOCK
        z = jnp.einsum('bhqd,bhkd->bhqk', q[:, :, q0:end], k[:, :, :end]).astype(jnp.float32) * scale
        qpos = q0 + jnp.arange(Q_BLOCK)[:, None]
        kpos = jnp.arange(end)[None, :]
        mask = kpos < qpos
        log_fail = jnp.where(mask, jax.nn.log_sigmoid(-z), 0.0)
        suffix = lax.cumsum(log_fail, axis=3, reverse=True) - log_fail
        a = jnp.where(mask, jnp.exp(jax.nn.log_sigmoid(z) + suffix), 0.0)
        outs.append(jnp.einsum('bhqk,bhkd->bhqd', a.astype(v.dtype), v[:, :, :end]))
    return jnp.concatenate(outs, axis=2)

def latent_attention(q_nope, q_rope, k_nope, k_rope, v):
    s_len = q_nope.shape[2]
    scale = (MLA_NOPE + MLA_ROPE) ** -0.5
    outs = []
    for blk in range(s_len // Q_BLOCK):
        q0 = blk * Q_BLOCK
        end = q0 + Q_BLOCK
        s_nope = jnp.einsum('bhqd,bhkd->bhqk', q_nope[:, :, q0:end], k_nope[:, :, :end])
        s_rope = jnp.einsum('bhqd,bkd->bhqk', q_rope[:, :, q0:end], k_rope[:, :end])
        s = (s_nope.astype(jnp.float32) + s_rope.astype(jnp.float32)) * scale
        qchunk = (q0 + jnp.arange(Q_BLOCK))[:, None] // CHUNK
        kchunk = jnp.arange(end)[None, :] // CHUNK
        s = jnp.where(kchunk <= qchunk, s, -jnp.inf)
        p = jax.nn.softmax(s, axis=-1)
        outs.append(jnp.einsum('bhqk,bhkd->bhqd', p.astype(v.dtype), v[:, :, :end]))
    return jnp.concatenate(outs, axis=2)

def causal_depthwise_conv(u, w, b):
    s_len = u.shape[1]
    up = jnp.pad(u, ((0, 0), (CONV_WIDTH - 1, 0), (0, 0)))
    acc = b + w[0] * up[:, 0:s_len]
    for i in range(1, CONV_WIDTH):
        acc = acc + w[i] * up[:, i:i + s_len]
    return acc

def hybrid_layer(x, cos, sin, norm1_g, w_in, b_gate, q_norm_g, w_uq, kv_norm_g, w_ukv,
                 w_proj_sb, w_proj_mla, w_out, norm2_g, w_up, conv_w, conv_b, w_down):
    b, s, _ = x.shape
    h = rms_norm(x, norm1_g)
    proj = h @ w_in
    cuts = [int(c) for c in np.cumsum(IN_SPLITS)[:-1]]
    sb_q, sb_k, sb_v, c_q, c_kv, k_rope, g_sb, g_mla = jnp.split(proj, cuts, axis=-1)

    o_sb = stick_breaking_attention(to_heads(sb_q, SB_HEADS), to_heads(sb_k, SB_HEADS),
                                    to_heads(sb_v, SB_HEADS))
    o_sb = from_heads(o_sb)

    q = to_heads(rms_norm(c_q, q_norm_g) @ w_uq, MLA_HEADS)
    q_nope, q_rope = q[..., :MLA_NOPE], apply_rope(q[..., MLA_NOPE:], cos, sin)
    kv = to_heads(rms_norm(c_kv, kv_norm_g) @ w_ukv, MLA_HEADS)
    k_nope, v = kv[..., :MLA_NOPE], kv[..., MLA_NOPE:]
    k_rope = apply_rope(k_rope, cos, sin)
    o_mla = from_heads(latent_attention(q_nope, q_rope, k_nope, k_rope, v))

    gate_sb = jax.nn.sigmoid(g_sb + b_gate[:D_MODEL])
    gate_mla = jax.nn.sigmoid(g_mla + b_gate[D_MODEL:])
    mixed = gate_sb * (o_sb @ w_proj_sb) + gate_mla * (o_mla @ w_proj_mla)
    x = x + mixed @ w_out

    h = rms_norm(x, norm2_g)
    u = causal_depthwise_conv(h @ w_up, conv_w, conv_b)
    gate, val = jnp.split(u, 2, axis=-1)
    x = x + (jax.nn.silu(gate) * val) @ w_down
    return x

def setup_inputs(seed: int = 0) -> dict:
    key = jax.random.key(seed)
    ks = jax.random.split(key, 20)
    f32 = jnp.float32

    def w(k, shape, fan_in):
        return jax.random.normal(k, shape, f32) * (fan_in ** -0.5)

    def gain(k, shape):
        return 1.0 + 0.02 * jax.random.normal(k, shape, f32)

    return {
        "x": jax.random.normal(ks[0], (BATCH, SEQ, D_MODEL), f32),
        "norm1_g": gain(ks[1], (DEPTH, D_MODEL)),
        "w_in": w(ks[2], (DEPTH, D_MODEL, IN_COLS), D_MODEL),
        "b_gate": 0.02 * jax.random.normal(ks[3], (DEPTH, 2 * D_MODEL), f32),
        "q_norm_g": gain(ks[4], (DEPTH, MLA_Q_LORA)),
        "w_uq": w(ks[5], (DEPTH, MLA_Q_LORA, MLA_HEADS * (MLA_NOPE + MLA_ROPE)), MLA_Q_LORA),
        "kv_norm_g": gain(ks[6], (DEPTH, MLA_KV_LORA)),
        "w_ukv": w(ks[7], (DEPTH, MLA_KV_LORA, MLA_HEADS * (MLA_NOPE + MLA_V)), MLA_KV_LORA),
        "w_proj_sb": w(ks[8], (DEPTH, SB_WIDTH, D_MODEL), SB_WIDTH),
        "w_proj_mla": w(ks[9], (DEPTH, MLA_HEADS * MLA_V, D_MODEL), MLA_HEADS * MLA_V),
        "w_out": w(ks[10], (DEPTH, D_MODEL, D_MODEL), D_MODEL),
        "norm2_g": gain(ks[11], (DEPTH, D_MODEL)),
        "w_up": w(ks[12], (DEPTH, D_MODEL, 2 * D_FF), D_MODEL),
        "conv_w": w(ks[13], (DEPTH, CONV_WIDTH, 2 * D_FF), CONV_WIDTH),
        "conv_b": 0.02 * jax.random.normal(ks[14], (DEPTH, 2 * D_FF), f32),
        "w_down": w(ks[15], (DEPTH, D_FF, D_MODEL), D_FF),
        "final_g": gain(ks[16], (D_MODEL,)),
    }

def reference(x, norm1_g, w_in, b_gate, q_norm_g, w_uq, kv_norm_g, w_ukv, w_proj_sb,
              w_proj_mla, w_out, norm2_g, w_up, conv_w, conv_b, w_down, final_g):
    cos, sin = rope_tables(x.shape[1], MLA_ROPE, x.dtype)
    for l in range(DEPTH):
        x = hybrid_layer(x, cos, sin, norm1_g[l], w_in[l], b_gate[l], q_norm_g[l], w_uq[l],
                         kv_norm_g[l], w_ukv[l], w_proj_sb[l], w_proj_mla[l], w_out[l],
                         norm2_g[l], w_up[l], conv_w[l], conv_b[l], w_down[l])
    return rms_norm(x, final_g)


_drawn_inputs = setup_inputs


def setup_inputs(seed=0):
    import zlib

    import numpy as np

    out = dict(_drawn_inputs(seed))
    spreads = {}
    factors = {'norm1_g': 4.087,
     'b_gate': 8.0,
     'q_norm_g': 8.0,
     'kv_norm_g': 8.0,
     'norm2_g': 2.808,
     'conv_b': 2.821,
     'final_g': 2.899}
    for name, (base, spread) in spreads.items():
        noise = np.random.default_rng([zlib.crc32(name.encode()), seed]).standard_normal(out[name].shape)
        drawn = base * np.exp(spread * noise) if base else spread * noise
        out[name] = __import__('jax').numpy.asarray(drawn.astype(out[name].dtype))
    for name, factor in factors.items():
        out[name] = (out[name] * factor).astype(out[name].dtype)
    return out
```

```python
from contextlib import ExitStack, contextmanager

import numpy as np

import concourse.bass as bass
from concourse import mybir

F32 = mybir.dt.float32
F32R = mybir.dt.float32r
ALU = mybir.AluOpType
ACT = mybir.ActivationFunctionType
AX = mybir.AxisListType

P = 128
L = 2
D = 2048
S = 256
DT = D // P
HEADS = 8
ROPE = 64
CQ, CKV = 768, 512
CQT, CKVT = CQ // P, CKV // P
FF = 5632
EPS = 1e-6
SB_SCALE = float(P) ** -0.5
MLA_SCALE = float(P + ROPE) ** -0.5
MASKED = -1e38

PARTS = (4, 4, 3)

RAW = 4
HIS = 4
AHEAD = 3
BANKS = 4
HALVES = 480
TILES = 272
CHUNKS = L * HALVES // 2
HALF_CREDIT = 8
TILE_CREDIT = 4
ACT_CREDIT = 4
ONE_UP = 1

N1, N2, CG, BG, CONV = 0, 16, 32, 42, 74
PCOLS = CONV + 32 * sum(PARTS)
COS, SIN, KEEP, SBNEG, MNEG, TRI, NEG, ONE, EYE = 0, 256, 512, 896, 1280, 1664, 1792, 1920, 2048
CCOLS = 2176


class Count:

    def __init__(self):
        self.const, self.terms = 0, []

    def at(self, k=0, div=1, mul=1, plus=0):
        v = ((self.const + k) // div) * mul + plus
        for reg, per in self.terms:
            assert per % div == 0
            v = reg * (per // div * mul) + v
        return v

    def up(self, n=1):
        self.const += n


@contextmanager
def loop(eng, trips, *counts):
    with eng.Fori(0, trips) as i:
        began = [c.const for c, _ in counts]
        for c, per in counts:
            c.terms.append((i, per))
        yield i
        for (c, per), b in zip(counts, began):
            assert c.const - b == per, (c.const - b, per)
            c.terms.pop()
            c.const = b + trips * per


def blocked(nk, nm, kb=4):
    return [(m, k) for b in range(0, nk, kb) for m in range(nm) for k in range(b, b + kb)]


def trunk(nc, x_in, stream, params, consts, y_out):
    ctx = ExitStack()
    with ctx:
        top = [16384]

        def at(name, shape, dt, offset):
            return nc.alloc_sbuf_tensor_at(name, shape, dt, offset=offset)

        def new(name, shape, dt=F32):
            o = top[0]
            size = 4 * int(np.prod(shape[1:]))
            top[0] = o + (size + 31) // 32 * 32
            return at(name, shape, dt, o), o

        x, _ = new("x", [P, DT, S])
        h, _ = new("h", [P, DT, 2 * S], F32R)
        raw, o = new("raw", [P, RAW, 16, P])
        lo = at("lo", [P, RAW, 16, P], F32R, o)
        hi, _ = new("hi", [P, HIS, 8, P], F32R)
        blend, r1 = new("blend", [P, 16, 2 * S], F32R)
        gates = at("gates", [P, 32, S], F32, r1)
        craw = at("craw", [P, CKVT + CQT, S], F32, r1)
        chl = at("chl", [P, CKVT + CQT, 2 * S], F32R, r1 + 4 * (CKVT + CQT) * S)
        sbqk, r2 = new("sbqk", [P, 16, S])
        osb = at("osb", [P, HEADS, 2 * S], F32R, r2)
        xsq = at("xsq", [P, DT, S], F32, r2)
        uconv = at("uconv", [P, 4, S + 8], F32, r2)
        fgate = at("fgate", [P, 4, S], F32, r2 + 4 * 4 * (S + 8))
        fval = at("fval", [P, 4, S], F32, r2 + 4 * 4 * (S + 8) + 4 * 4 * S)
        v, r3 = new("v", [P, 2, 1024])
        sig = at("sig", [P, 4, 2 * S], F32, r3)
        mqk, r4 = new("mqk", [P, 16, S])
        omla = at("omla", [P, HEADS, 2 * S], F32R, r4)
        qr, _ = new("qr", [P, HEADS // 2, S])
        kr, _ = new("kr", [P, S])
        mv, r5 = new("mv", [P, 2, 1024])
        psb = at("psb", [P, 4, S], F32, r5)
        pmla = at("pmla", [P, 4, S], F32, r5 + 4 * 4 * S)

        k_st, _ = new("k_st", [P, S])
        v_st, _ = new("v_st", [P, 2, P])
        qn_st, o = new("qn_st", [P, S])
        swap = at("swap", [P, S], F32, o)
        qr_st, _ = new("qr_st", [P, S])
        mv_st, _ = new("mv_st", [P, 2, P])
        tmp, _ = new("tmp", [P, 2, S])
        sp, o = new("sp", [P, 384])
        rstd_kv = at("rstd_kv", [P, S], F32, o)
        wgt, o = new("wgt", [P, 384])
        sqsum = at("sqsum", [P, S], F32, o)
        prob, o = new("prob", [P, 384])
        probT, _ = new("probT", [P, 384])
        sq = at("sq", [P, 2, S], F32, o)
        rstd_q = at("rstd_q", [P, S], F32, o + 4 * 2 * S)
        rstd, _ = new("rstd", [P, S])
        cst, _ = new("cst", [P, CCOLS])
        par, _ = new("par", [P, L * PCOLS + DT])
        norms, _ = new("norms", [P, BG])
        bias8, _ = new("bias8", [P, 8])
        gain4, _ = new("gain4", [P, 4])
        taps_g, _ = new("taps_g", [P, 16])
        taps_v, _ = new("taps_v", [P, 16])
        stat, _ = new("stat", [P, 8])
        rstd_tok, _ = new("rstd_tok", [P, 2])
        rstd_kv_tok, _ = new("rstd_kv_tok", [P, 2])
        assert top[0] <= 229344, top[0]

        def c_(a, n=P):
            return cst[:, a:a + n]

        def bank(name):
            return ctx.enter_context(nc.psum_tensor(name, [P, 512], F32))

        res = [bank(f"res{b}") for b in range(BANKS)]
        p_sb, p_ml, p_tr, p_st = bank("p_sb"), bank("p_ml"), bank("p_tr"), bank("p_st")

        def sem(name):
            return ctx.enter_context(nc.semaphore(name))

        landed = [sem(f"landed{s}") for s in range(RAW)]
        hi_done = sem("hi_done")
        split_done = sem("split_done")
        halves_used = sem("halves_used")
        tiles_done = sem("tiles_done")
        tmp_ready = sem("tmp_ready")
        tiles_free = sem("tiles_free")
        const_in, y_out_sem = sem("const_in"), sem("y_out_sem")
        cst_in = sem("cst_in")
        x_landed = [sem(f"x_landed{q}") for q in range(4)]
        x_done = sem("x_done")
        dve_step, act_step, pool_step = sem("dve_step"), sem("act_step"), sem("pool_step")
        sq_ready = sem("sq_ready")
        sq_added = sem("sq_added")
        sum_done = sem("sum_done")
        rstd_ready = sem("rstd_ready")
        scaled = sem("scaled")
        h_hi = sem("h_hi")
        h_ready = sem("h_ready")
        c_hi, c_ready = sem("c_hi"), sem("c_ready")
        gain_in = sem("gain_in")
        xsq_ready = sem("xsq_ready")
        rope_done = sem("rope_done")
        bias_in = sem("bias_in")
        taps_in = sem("taps_in")
        k_staged, staged = sem("k_staged"), sem("staged")
        z_done, ln_done, sp_ready, p_done = sem("z_done"), sem("ln_done"), sem("sp_ready"), sem("p_done")
        logw_ready, w_ready, osb_done = sem("logw_ready"), sem("w_ready"), sem("osb_done")
        osb_hi, osb_free = sem("osb_hi"), sem("osb_free")
        s_done, max_ready, exp_done, prob_ready = sem("s_done"), sem("max_ready"), sem("exp_done"), sem("prob_ready")
        tr_done, tr_copied, om_done = sem("tr_done"), sem("tr_copied"), sem("om_done")
        om_hi, om_free = sem("om_hi"), sem("om_free")
        sig_done, psb_gated, mix_f32, mix_hi, mix_ready = (
            sem("sig_done"), sem("psb_gated"), sem("mix_f32"), sem("mix_hi"), sem("mix_ready"))
        tap2_done, conv_done, silu_done, ffn_f32, ffn_hi, ffn_ready = (
            sem("tap2_done"), sem("conv_done"), sem("silu_done"), sem("ffn_f32"), sem("ffn_hi"), sem("ffn_ready"))

        SCALED = 16 + 11 + HEADS + 12 + 2 * DT + 2 * (FF // P)
        SUMS = 4
        SQUARES = CKVT + CQT + 2 * DT

        block = ctx.enter_context(nc.Block())

        @block.sync
        def _(sp_):
            sp_.dma_start(par[:, :], params).then_inc(const_in, 16)
            for q in range(4):
                sp_.dma_start(x[:, 4 * q:4 * q + 4, :], x_in[:, 4 * q:4 * q + 4, :]).then_inc(x_landed[q], 16)
            sp_.dma_start(cst[:, :], consts).then_inc(cst_in, 16)
            with sp_.Fori(0, CHUNKS // RAW) as i:
                for s in range(RAW):
                    sp_.wait_ge(halves_used, i * (2 * RAW) + (2 * s - 2 * RAW + 3 + HALF_CREDIT))
                    sp_.dma_start(raw[:, s, :, :], stream[i * RAW + s]).then_inc(landed[s], 16)
            for s in range(2):
                sp_.wait_ge(halves_used, 2 * (CHUNKS + s) - 2 * RAW + 3 + HALF_CREDIT)
                sp_.dma_start(raw[:, s, :, :], stream[CHUNKS + s]).then_inc(landed[s], 16)
            for q in range(4):
                sp_.wait_ge(x_done, q + 1)
                sp_.dma_start(y_out[:, 4 * q:4 * q + 4, :], x[:, 4 * q:4 * q + 4, :]).then_inc(y_out_sem, 16)
            sp_.wait_ge(y_out_sem, 64)
            for s in range(RAW):
                sp_.wait_ge(landed[s], 16 * (CHUNKS // RAW + (s < 2)))

        @block.tensor
        def _(pe):
            U, T, HD = Count(), Count(), Count()
            pe.sem_inc(halves_used, HALF_CREDIT)
            for started in (z_done, om_done, sum_done):
                pe.sem_inc(started, ONE_UP)

            def half_ready():
                pe.wait_ge(split_done, U.at(1))

            def w_tile(idx):
                u = U.const
                return hi[:, u % HIS, idx, :], lo[:, u // 2 % RAW, 8 * (u % 2) + idx, :]

            def gemm(seq, nk, moving, ready=None, last_tile_inc=1, last_half_inc=1):
                for s, (m, k) in enumerate(seq):
                    idx = s % 8
                    if idx == 0:
                        half_ready()
                    if k == 0:
                        pe.wait_ge(tiles_free, T.at(m + 1))
                    if ready and k % 4 == 0 and m == seq[0][0]:
                        ready(k)
                    out = res[(T.const + m) % BANKS]
                    w_hi, w_lo = w_tile(idx)
                    end = s == len(seq) - 1
                    a = pe.matmul(out[:, :], w_hi, moving(k), start=(k == 0), stop=(k == nk - 1), skip_group_check=True)
                    b = pe.matmul(out[:, 0:S], w_lo, moving(k)[:, 0:S], start=False, stop=(k == nk - 1), skip_group_check=True)
                    if idx == 7 or end:
                        a.then_inc(halves_used, last_half_inc if end else 1)
                        U.up(last_half_inc if end else 1)
                    if k == nk - 1:
                        b.then_inc(tiles_done, last_tile_inc if end else 1)

            def gemm_tokens(nk, acts, ready=None):
                for kp in range(nk // 2):
                    half_ready()
                    if ready and kp % 2 == 0:
                        ready(2 * kp)
                    for blk in range(2):
                        out = res[(T.const + blk) % BANKS]
                        if kp == 0:
                            pe.wait_ge(tiles_free, T.at(blk + 1))
                        for j in range(2):
                            k = 2 * kp + j
                            u = U.const
                            w_hi = hi[:, u % HIS, 4 * j:4 * j + 4, :]
                            w_lo = lo[:, u // 2 % RAW, 8 * (u % 2) + 4 * j:8 * (u % 2) + 4 * j + 4, :]
                            a_hi = acts(k)[:, blk * P:blk * P + P]
                            a_lo = acts(k)[:, S + blk * P:S + blk * P + P]
                            pe.matmul(out[:, :], a_hi, w_hi, start=(k == 0), stop=False, skip_group_check=True)
                            a = pe.matmul(out[:, :], a_lo, w_hi, start=False, stop=False, skip_group_check=True)
                            b = pe.matmul(out[:, :], a_hi, w_lo, start=False, stop=(k == nk - 1), skip_group_check=True)
                            if blk == 1 and j == 1:
                                a.then_inc(halves_used, 1)
                            if k == nk - 1:
                                b.then_inc(tiles_done, 1)
                    U.up()
                T.up(2)

            def norm_sum(number, squares, tokens=False):
                pe.wait_ge(sq_added, squares)
                pe.wait_ge(rstd_ready, number + ONE_UP)
                if tokens:
                    for b in range(2):
                        pe.matmul(p_st[:, S + b:S + b + 1], sqsum[:, b * P:b * P + P], c_(ONE, 1),
                                  start=(b == 0), stop=True, skip_group_check=True)
                pe.matmul(p_st[:, 0:S], c_(ONE), sqsum[:, :], start=not tokens, stop=True,
                          skip_group_check=True).then_inc(sum_done, 1)

            def H(k):
                return h[:, k, :]

            def C(k):
                return chl[:, k, :]

            def B(k):
                return blend[:, k, :]

            def attention_scores(i, e):
                pe.wait_ge(k_staged, HD.at(1))
                pe.wait_ge(osb_free, HD.at() + ONE_UP)
                q = sbqk[:, bass.ds(i * 4 + 2 * e, 1), :].rearrange("p a t -> p (a t)")
                pe.matmul(p_sb[:, 0:S], k_st[:, 0:P], q, start=True, stop=True, skip_group_check=True)
                pe.matmul(p_sb[:, S:384], k_st[:, P:S], q[:, P:S], start=False, stop=True,
                          skip_group_check=True).then_inc(z_done, 1)
                pe.wait_ge(staged, HD.at(1))
                pe.wait_ge(om_free, HD.at() + ONE_UP)
                kn = mqk[:, bass.ds(i * 4 + 2 * e + 1, 1), :].rearrange("p a t -> p (a t)")
                r = slice(64 * e, 64 * e + 64)
                pe.matmul(p_ml[:, 0:P], qn_st[:, 0:P], kn[:, 0:P], start=True, stop=False, skip_group_check=True)
                pe.matmul(p_ml[:, 0:P], qr_st[r, 0:P], kr[r, 0:P], start=False, stop=True, skip_group_check=True)
                pe.matmul(p_ml[:, P:384], qn_st[:, P:S], kn, start=False, stop=False, skip_group_check=True)
                pe.matmul(p_ml[:, P:384], qr_st[r, P:S], kr[r, :], start=False, stop=True,
                          skip_group_check=True).then_inc(s_done, 1)

            def attention_weights():
                pe.wait_ge(sp_ready, HD.at(1))
                pe.matmul(p_sb[:, 0:S], c_(TRI), sp[:, 0:S], start=False, stop=True, skip_group_check=True)
                pe.matmul(p_sb[:, P:S], c_(NEG), sp[:, S:384], start=False, stop=True, skip_group_check=True)
                pe.matmul(p_sb[:, S:384], c_(TRI), sp[:, S:384], start=False, stop=True,
                          skip_group_check=True).then_inc(p_done, 1)
                pe.wait_ge(prob_ready, HD.at(1))
                for b in range(3):
                    t = pe.transpose(p_tr[:, b * P:b * P + P], prob[:, b * P:b * P + P], c_(EYE))
                t.then_inc(tr_done, 1)

            def attention_values():
                pe.wait_ge(w_ready, HD.at(1))
                pe.matmul(p_sb[:, 0:S], v_st[:, 0, :], wgt[:, 0:S], start=True, stop=True, skip_group_check=True)
                pe.matmul(p_sb[:, P:S], v_st[:, 1, :], wgt[:, S:384], start=False, stop=True,
                          skip_group_check=True).then_inc(osb_done, 1)
                pe.wait_ge(tr_copied, HD.at(1))
                pe.matmul(p_ml[:, 0:S], mv_st[:, 0, :], probT[:, 0:S], start=True, stop=True, skip_group_check=True)
                pe.matmul(p_ml[:, P:S], mv_st[:, 1, :], probT[:, S:384], start=False, stop=True,
                          skip_group_check=True).then_inc(om_done, 1)
                HD.up()

            four = blocked(16, 4)
            pe.wait_ge(cst_in, 16)
            with loop(pe, L, (U, HALVES), (T, TILES), (HD, HEADS)) as l:
                def first_h(k):
                    pe.wait_ge(h_ready, l * (2 * DT) + (k + 4))

                def second_h(k):
                    pe.wait_ge(h_ready, l * (2 * DT) + (DT + k + 4))

                gemm(four[:48], 16, H, first_h)
                norm_sum(l * SUMS, l * SQUARES + DT, tokens=True)
                gemm(four[48:], 16, H, lambda k: first_h(12))
                T.up(4)
                with loop(pe, 3, (U, 8), (T, 4)):
                    gemm(four, 16, H)
                    T.up(4)
                for _ in range(2):
                    gemm_tokens(16, H)
                gemm(four, 16, H)
                T.up(4)
                gemm(four[:32], 16, H)
                norm_sum(l * SUMS + 1, l * SQUARES + DT + CKVT, tokens=True)
                gemm(four[32:], 16, H)
                T.up(4)
                gemm(blocked(16, 3), 16, H, last_tile_inc=2)
                T.up(4)
                pe.wait_ge(c_ready, l * 3 + 1)
                for _ in range(2):
                    gemm(blocked(4, 4), 4, C)
                    T.up(4)
                gemm_tokens(4, C)
                norm_sum(l * SUMS + 2, l * SQUARES + DT + CKVT + CQT)
                gemm_tokens(4, C)
                pe.wait_ge(c_ready, l * 3 + 3)
                gemm(blocked(CQT, 12, CQT), CQT, lambda k: C(CKVT + k), last_half_inc=2)
                T.up(12)
                with loop(pe, HEADS // 2, (U, 16), (T, 8), (HD, 2)) as i:
                    for e in range(2):
                        gemm(four[:16], 16, H)
                        attention_scores(i, e)
                        gemm(four[16:48], 16, H)
                        attention_weights()
                        gemm(four[48:], 16, H)
                        attention_values()
                        T.up(4)
                with loop(pe, 4, (U, 8), (T, 8)):
                    pe.wait_ge(osb_free, l * HEADS + HEADS + ONE_UP)
                    gemm(blocked(8, 4), 8, lambda k: osb[:, k, :])
                    T.up(4)
                    pe.wait_ge(om_free, l * HEADS + HEADS + ONE_UP)
                    gemm(blocked(8, 4), 8, lambda k: omla[:, k, :])
                    T.up(4)
                with loop(pe, 4, (U, 8), (T, 4)):
                    gemm(four, 16, B, lambda k: pe.wait_ge(mix_ready, l * DT + (k + 4)))
                    T.up(4)
                done = 0
                for part, groups in enumerate(PARTS):
                    if part == 0:
                        gemm(four[:48], 16, H, second_h)
                        norm_sum(l * SUMS + 3, l * SQUARES + DT + CKVT + CQT + DT)
                        gemm(four[48:], 16, H, lambda k: second_h(12))
                    else:
                        gemm(four, 16, H)
                    T.up(4)
                    with loop(pe, groups - 1, (U, 16), (T, 8)):
                        for _ in range(2):
                            gemm(four, 16, H)
                            T.up(4)
                    gemm(four, 16, H)
                    T.up(4)

                    def ffn_in(k, done=done):
                        pe.wait_ge(ffn_ready, l * (FF // P) + (done + k + 4 + ACT_CREDIT))

                    nk = 4 * groups
                    if nk == 16:
                        with loop(pe, 4, (U, 8), (T, 4)):
                            gemm(four, 16, B, ffn_in)
                            T.up(4)
                    else:
                        for _ in range(4):
                            gemm(blocked(nk, 4), nk, B, ffn_in)
                            T.up(4)
                    done += nk
            norm_sum(L * SUMS, L * SQUARES + DT)

        @block.scalar
        def _(act):
            U, T, HD, N, G, FT, FG, FP, SQ, W, X = (Count() for _ in range(11))

            def split(k=AHEAD):
                u = U.const + k
                if u % 2 == 0:
                    act.wait_ge(landed[u // 2 % RAW], U.at(k, 8, 16, 16))
                act.wait_ge(halves_used, U.at(k + 1 - HIS + HALF_CREDIT))
                act.activation(hi[:, u % HIS, :, :], raw[:, u // 2 % RAW, 8 * (u % 2):8 * (u % 2) + 8, :],
                               ACT.Copy).then_inc(hi_done, 1)

            def halves(n):
                for _ in range(n):
                    split()
                    U.up()

            def take(last=1):
                act.wait_ge(tiles_done, T.at(1))
                act.wait_ge(tiles_free, T.at(3))
                act.activation(tmp[:, T.const % 2, :], res[T.const % BANKS][:, S:2 * S], ACT.Copy).then_inc(tmp_ready, last)
                T.up(last)

            def square(src):
                act.wait_ge(sq_added, SQ.at(-1))
                act.activation(sq[:, SQ.const % 2, :], src, ACT.Square).then_inc(sq_ready, 1)
                SQ.up()

            def make_rstd(n, dst, tokens=None):
                act.wait_ge(sum_done, N.at(1) + ONE_UP)
                N.up()
                if tokens is not None:
                    act.activation(tokens[:, :], p_st[:, S:S + 2], ACT.Ln, scale=1.0 / n, bias=EPS)
                act.activation(dst[:, :], p_st[:, 0:S], ACT.Ln, scale=1.0 / n, bias=EPS).then_inc(act_step, 1)
                STEP.up()
                act.wait_ge(act_step, STEP.at())
                if tokens is not None:
                    act.activation(tokens[:, :], tokens[:, :], ACT.Exp, scale=-0.5)
                act.activation(dst[:, :], dst[:, :], ACT.Exp, scale=-0.5).then_inc(rstd_ready, 1)

            def flat(t):
                return t.rearrange("p a t -> p (a t)")

            STEP = Count()
            act.sem_inc(rstd_ready, ONE_UP)
            act.sem_inc(sq_ready, DT)
            SQ.up(DT)
            act.wait_ge(const_in, 16)
            for q in range(4):
                act.wait_ge(x_landed[q], 16)
                for k in range(4 * q, 4 * q + 4):
                    act.activation(h[:, k, 0:S], x[:, k, :], ACT.Copy, scale=par[:, N1 + k:N1 + k + 1]).then_inc(h_hi, 1)
                if q < AHEAD:
                    split(q)
            for q in range(4):
                act.activation(xsq[:, 4 * q:4 * q + 4, :], x[:, 4 * q:4 * q + 4, :], ACT.Square).then_inc(xsq_ready, 1)
            act.activation(stat[:, 6:7], par[:, 0:1], ACT.Exp)
            with loop(act, L, (U, HALVES), (T, TILES), (HD, HEADS), (N, SUMS), (G, DT), (FT, 2 * FF // P),
                      (FG, FF // P), (FP, FF // P), (SQ, SQUARES), (STEP, ACT_STEPS), (W, SCALED), (X, 2 * DT)) as l:
                act.wait_ge(h_ready, X.at(DT))
                act.activation(norms[:, N2:BG], par[:, bass.ds(l * PCOLS + N2, BG - N2)], ACT.Copy).then_inc(gain_in, 1)

                def four_tiles():
                    for _ in range(2):
                        split()
                        take()
                        take()
                        U.up()

                halves(4)
                act.wait_ge(scaled, W.at() + ONE_UP)
                make_rstd(D, rstd, rstd_tok)
                halves(2)
                four_tiles()
                W.up(4)
                with loop(act, 3, (U, 8), (T, 4), (W, 4)):
                    halves(6)
                    four_tiles()
                    W.up(4)

                def token_tiles(dst, cg, n, factor):
                    halves(n)
                    for blk in range(2):
                        act.wait_ge(tiles_done, T.at(1))
                        act.activation(dst[:, blk, 512 * cg:512 * cg + S], res[T.const % BANKS][:, 0:S], ACT.Copy,
                                       scale=factor[:, blk:blk + 1]).then_inc(tmp_ready, 1)
                        T.up()

                for cg in range(2):
                    token_tiles(v, cg, 8, rstd_tok)

                def c_tiles(first, n):
                    for k in range(first, first + n):
                        W.up()
                        act.wait_ge(scaled, W.at() + ONE_UP)
                        square(craw[:, k, :])
                        act.wait_ge(gain_in, l * 2 + 1)
                        hi_of = act.activation(chl[:, k, 0:S], craw[:, k, :], ACT.Copy, scale=norms[:, CG + k:CG + k + 1])
                    hi_of.then_inc(c_hi, 1)

                halves(6)
                four_tiles()
                split()
                c_tiles(0, 4)
                U.up()
                halves(3)
                make_rstd(CKV, rstd_kv, rstd_kv_tok)
                halves(2)
                four_tiles()
                split()
                c_tiles(CKVT, 4)
                U.up()
                halves(3)
                split()
                take()
                U.up()
                split()
                take()
                U.up()
                take(2)
                split()
                c_tiles(CKVT + 4, 2)
                W.up()
                take()
                take()
                U.up()
                for half in range(3):
                    split()
                    take()
                    take()
                    U.up()
                W.up(8)
                token_tiles(mv, 0, 2, rstd_kv_tok)
                make_rstd(CQ, rstd_q)
                token_tiles(mv, 1, 2, rstd_kv_tok)
                at_tile = 0
                for u in range(10):
                    split()
                    U.up()
                    while at_tile < 12 and 6 * (at_tile + 1) <= 8 * (u + 1):
                        take()
                        at_tile += 1
                W.up(12)
                with loop(act, HEADS // 2, (U, 16), (T, 8), (HD, 2), (STEP, 4), (W, 8)) as i:
                    for e in range(2):
                        split()
                        U.up()
                        act.wait_ge(z_done, HD.at() + ONE_UP)
                        act.activation(k_st[:, :], flat(sbqk[:, bass.ds(i * 4 + 2 * e + 1, 1), :]), ACT.Copy,
                                       scale=SB_SCALE).then_inc(k_staged, 1)
                        split()
                        U.up()
                        split()
                        U.up()
                        act.wait_ge(scaled, W.at() + ONE_UP)
                        act.wait_ge(z_done, HD.at(1) + ONE_UP)
                        act.activation(sp[:, :], p_sb[:, 0:384], ACT.Abs).then_inc(act_step, 1)
                        act.wait_ge(act_step, STEP.at(1))
                        act.activation(sp[:, :], sp[:, :], ACT.Exp, scale=-1.0).then_inc(act_step, 1)
                        act.wait_ge(act_step, STEP.at(2))
                        STEP.up(2)
                        act.activation(sp[:, :], sp[:, :], ACT.Ln, bias=1.0).then_inc(ln_done, 1)
                        split()
                        U.up()
                        act.wait_ge(max_ready, HD.at(1))
                        act.activation(prob[:, 0:P], prob[:, 0:P], ACT.Exp, bias=stat[:, 2:3], accum_out=stat[:, 4:5])
                        act.activation(prob[:, P:384], prob[:, P:384], ACT.Exp, bias=stat[:, 3:4],
                                       accum_out=stat[:, 5:6]).then_inc(exp_done, 1)
                        halves(2)
                        split()
                        act.wait_ge(logw_ready, HD.at(1))
                        act.activation(wgt[:, :], wgt[:, :], ACT.Exp).then_inc(w_ready, 1)
                        act.wait_ge(tr_done, HD.at(1))
                        act.activation(probT[:, :], p_tr[:, 0:384], ACT.Copy).then_inc(tr_copied, 1)
                        take()
                        take()
                        U.up()
                        split()
                        take()
                        take()
                        U.up()
                        act.wait_ge(osb_done, HD.at(1))
                        act.activation(flat(osb[:, bass.ds(i * 2 + e, 1), 0:S]), p_sb[:, 0:S], ACT.Copy).then_inc(osb_hi, 1)
                        act.wait_ge(om_done, HD.at(1) + ONE_UP)
                        act.activation(flat(omla[:, bass.ds(i * 2 + e, 1), 0:S]), p_ml[:, 0:S], ACT.Copy).then_inc(om_hi, 1)
                        HD.up()
                        W.up(4)
                act.activation(stat[:, 6:7], cst[:, ONE:ONE + 1], ACT.Sigmoid)
                with loop(act, 4, (U, 8), (T, 8), (G, 4), (STEP, 1)) as i:
                    act.activation(bias8[:, :], par[:, bass.ds(l * PCOLS + i * 8 + BG, 8)], ACT.Copy).then_inc(act_step, 1)
                    STEP.up()
                    act.wait_ge(scaled, W.at() + ONE_UP)
                    act.wait_ge(act_step, STEP.at())
                    for m in range(4):
                        if m < 2:
                            halves(1)
                        for w in range(2):
                            sg = act.activation(sig[:, m, w * S:w * S + S], flat(gates[:, bass.ds(i * 8 + 2 * m + w, 1), :]),
                                                ACT.Sigmoid, bias=bias8[:, 2 * m + w:2 * m + w + 1])
                        sg.then_inc(sig_done, 1)
                    four_tiles()
                    halves(2)

                    def mixed(n):
                        for m in range(n, n + 2):
                            act.wait_ge(mix_f32, G.at(1))
                            act.activation(flat(blend[:, bass.ds(i * 4 + m, 1), 0:S]), pmla[:, m, :],
                                           ACT.Copy).then_inc(mix_hi, 1)
                            G.up()

                    split()
                    take()
                    take()
                    U.up()
                    split()
                    take()
                    take()
                    mixed(0)
                    U.up()
                    mixed(2)

                def residual_tiles(i, next_norm, nhalves=6, gain=None):
                    def post(n):
                        for m in range(n, n + 2) if next_norm else ():
                            k = i * 4 + m
                            act.wait_ge(tiles_free, T.at(TILE_CREDIT - 1 + m - n))
                            square(flat(x[:, bass.ds(k, 1), :]))
                            g = gain4[:, m:m + 1] if gain is None else norms[:, gain + k:gain + k + 1]
                            act.activation(flat(h[:, bass.ds(k, 1), 0:S]), flat(x[:, bass.ds(k, 1), :]), ACT.Copy,
                                           scale=g).then_inc(h_hi, 1)
                            X.up()

                    halves(nhalves)
                    split()
                    take()
                    take()
                    U.up()
                    split()
                    post(0)
                    take()
                    take()
                    U.up()
                    post(2)

                with loop(act, 4, (U, 8), (T, 4), (SQ, 4), (STEP, 1), (X, 4)) as i:
                    act.wait_ge(h_ready, X.at(DT))
                    act.activation(gain4[:, :], norms[:, bass.ds(i * 4 + N2, 4)], ACT.Copy).then_inc(act_step, 1)
                    STEP.up()
                    act.wait_ge(act_step, STEP.at())
                    residual_tiles(i, True)
                act.activation(norms[:, 0:DT], par[:, bass.ds(l * PCOLS + PCOLS, DT)], ACT.Copy).then_inc(gain_in, 1)

                def load_taps(dst, i, value, first):
                    act.wait_ge(conv_done, FT.at() + ONE_UP)
                    act.activation(dst[:, :], par[:, bass.ds(l * PCOLS + i * 32 + (CONV + 32 * first + 16 * value), 16)],
                                   ACT.Copy).then_inc(taps_in, 1)

                def tap2(m, dst, taps):
                    W.up()
                    act.wait_ge(scaled, W.at() + ONE_UP)
                    act.activation(dst[:, m, :], uconv[:, m, 2:2 + S], ACT.Identity, scale=taps[:, 4 * m + 2:4 * m + 3],
                                   bias=taps[:, 4 * m + 3:4 * m + 4]).then_inc(tap2_done, 1)
                    FT.up()

                def silu(m):
                    act.wait_ge(conv_done, FT.at(m - 3) + ONE_UP)
                    act.activation(fgate[:, m, :], fgate[:, m, :], ACT.Silu).then_inc(silu_done, 1)
                    FG.up()

                def product_hi(i, m):
                    act.wait_ge(ffn_f32, FP.at(1))
                    act.activation(flat(blend[:, bass.ds(i * 4 + m, 1), 0:S]), fgate[:, m, :], ACT.Copy).then_inc(ffn_hi, 1)
                    FP.up()

                def gate_group(i, first, part_start):
                    split()
                    if not part_start:
                        for m in range(2):
                            product_hi(i - 1, m)
                    U.up()
                    split()
                    if not part_start:
                        for m in range(2, 4):
                            product_hi(i - 1, m)
                    U.up()
                    if part_start and first == 0:
                        halves(2)
                        act.wait_ge(scaled, W.at() + ONE_UP)
                        make_rstd(D, rstd)
                        act.activation(stat[:, 6:7], cst[:, ONE:ONE + 1], ACT.Silu)
                        halves(2)
                    else:
                        halves(4)
                    load_taps(taps_g, i, 0, first)
                    split()
                    take()
                    take()
                    U.up()
                    split()
                    act.wait_ge(ffn_ready, FP.at(ACT_CREDIT))
                    act.wait_ge(taps_in, FT.at(4, 4, 1))
                    tap2(0, fgate, taps_g)
                    tap2(1, fgate, taps_g)
                    take()
                    take()
                    U.up()

                def value_group(i, first):
                    split()
                    tap2(2, fgate, taps_g)
                    tap2(3, fgate, taps_g)
                    U.up()
                    split()
                    for m in range(4):
                        silu(m)
                    U.up()
                    halves(4)
                    load_taps(taps_v, i, 1, first)
                    split()
                    take()
                    take()
                    U.up()
                    split()
                    act.wait_ge(taps_in, FT.at(4, 4, 1))
                    tap2(0, fval, taps_v)
                    tap2(1, fval, taps_v)
                    take()
                    take()
                    U.up()
                    tap2(2, fval, taps_v)
                    tap2(3, fval, taps_v)

                first = 0
                for groups in PARTS:
                    gate_group(0, first, True)
                    with loop(act, groups - 1, (U, 16), (T, 8), (FT, 8), (FG, 4), (FP, 4), (W, 8)) as i:
                        value_group(i, first)
                        gate_group(i + 1, first, False)
                    value_group(groups - 1, first)
                    for m in range(4):
                        product_hi(groups - 1, m)
                    first += groups
                    if groups == 4:
                        with loop(act, 4, (U, 8), (T, 4)) as i:
                            residual_tiles(i, False)
                    else:
                        act.wait_ge(gain_in, l * 2 + 2)
                        for i in range(4):
                            residual_tiles(i, True, 4, N1)
                act.activation(stat[:, 6:7], cst[:, ONE:ONE + 1], ACT.Exp)
            act.wait_ge(scaled, W.at() + ONE_UP)
            make_rstd(D, rstd)

        @block.vector
        def _(dve):
            U, T, HD, N, G, FT, FP, STEP, X = (Count() for _ in range(9))
            dve.sem_inc(tiles_free, TILE_CREDIT)
            dve.sem_inc(ffn_ready, ACT_CREDIT)
            for started in (osb_free, om_free, conv_done):
                dve.sem_inc(started, ONE_UP)

            def flat(t):
                return t.rearrange("p a t -> p (a t)")

            def step(ins):
                ins.then_inc(dve_step, 1)
                STEP.up()
                dve.wait_ge(dve_step, STEP.at())

            def split(k=AHEAD):
                u = U.const + k
                part = slice(8 * (u % 2), 8 * (u % 2) + 8)
                dve.wait_ge(hi_done, U.at(k + 1))
                dve.tensor_tensor(lo[:, u // 2 % RAW, part, :], raw[:, u // 2 % RAW, part, :],
                                  hi[:, u % HIS, :, :].bitcast(F32), ALU.subtract).then_inc(split_done, 1)

            def halves(n):
                for _ in range(n):
                    split()
                    U.up()

            def join(dst, last=1):
                dve.wait_ge(tmp_ready, T.at(1))
                dve.tensor_tensor(dst, res[T.const % BANKS][:, 0:S], tmp[:, T.const % 2, :], ALU.add).then_inc(tiles_free, last)
                T.up(last)

            def low_h(k, gain):
                dve.wait_ge(h_hi, X.at(1))
                dve.scalar_tensor_tensor(out=flat(h[:, bass.ds(k, 1), S:2 * S]), in0=flat(x[:, bass.ds(k, 1), :]),
                                         scalar=gain, in1=flat(h[:, bass.ds(k, 1), 0:S].bitcast(F32)),
                                         op0=ALU.mult, op1=ALU.subtract).then_inc(h_ready, 1)
                X.up()

            dve.wait_ge(const_in, 16)
            for q in range(4):
                for k in range(4 * q, 4 * q + 4):
                    low_h(k, par[:, N1 + k:N1 + k + 1])
                if q < AHEAD:
                    split(q)
            dve.wait_ge(xsq_ready, 2)
            dve.tensor_tensor(xsq[:, 0:4, :], xsq[:, 0:4, :], xsq[:, 4:8, :], ALU.add)
            dve.wait_ge(xsq_ready, 4)
            step(dve.tensor_tensor(xsq[:, 8:12, :], xsq[:, 8:12, :], xsq[:, 12:16, :], ALU.add))
            step(dve.tensor_tensor(xsq[:, 0:4, :], xsq[:, 0:4, :], xsq[:, 8:12, :], ALU.add))
            step(dve.tensor_tensor(xsq[:, 0:2, :], xsq[:, 0:2, :], xsq[:, 2:4, :], ALU.add))
            dve.tensor_tensor(sqsum[:, :], xsq[:, 0, :], xsq[:, 1, :], ALU.add).then_inc(sq_added, DT)
            dve.wait_ge(cst_in, 16)
            with loop(dve, L, (U, HALVES), (T, TILES), (HD, HEADS), (N, SUMS), (G, DT), (FT, 2 * FF // P),
                      (FP, FF // P), (STEP, DVE_STEPS), (X, 2 * DT)) as l:
                def four_tiles(dst):
                    for pair in range(2):
                        split()
                        for m in range(2):
                            join(dst(2 * pair + m))
                        U.up()

                def qk(i):
                    halves(6)
                    four_tiles(lambda m: flat(sbqk[:, bass.ds(i * 4 + m, 1), :]))

                qk(0)
                with loop(dve, 3, (U, 8), (T, 4)) as i:
                    qk(i + 1)

                def token_tiles(dst, cg, n, factor):
                    halves(n)
                    for blk in range(2):
                        dve.wait_ge(tmp_ready, T.at(1))
                        dve.tensor_scalar(dst[:, blk, 512 * cg + S:512 * cg + 2 * S], res[T.const % BANKS][:, S:2 * S],
                                          factor[:, blk:blk + 1], None, ALU.mult).then_inc(tiles_free, 1)
                        T.up()

                def low_c(first, n, number):
                    dve.wait_ge(c_hi, number)
                    for k in range(first, first + n):
                        ins = dve.scalar_tensor_tensor(out=chl[:, k, S:2 * S], in0=craw[:, k, :],
                                                       scalar=norms[:, CG + k:CG + k + 1],
                                                       in1=chl[:, k, 0:S].bitcast(F32), op0=ALU.mult, op1=ALU.subtract)
                    ins.then_inc(c_ready, 1)

                for cg in range(2):
                    token_tiles(v, cg, 8, rstd_tok)
                halves(6)
                four_tiles(lambda m: craw[:, m, :])
                halves(2)
                low_c(0, 4, l * 3 + 1)
                halves(4)
                four_tiles(lambda m: craw[:, CKVT + m, :])
                halves(2)
                low_c(CKVT, 4, l * 3 + 2)
                halves(2)
                split()
                join(craw[:, CKVT + 4, :])
                U.up()
                split()
                join(craw[:, CKVT + 5, :])
                U.up()
                join(kr[:, :], 2)
                four_tiles(lambda m: mqk[:, 2 * m + 1, :])
                low_c(CKVT + 4, 2, l * 3 + 3)
                four_tiles(lambda m: mqk[:, 2 * (4 + m) + 1, :])
                token_tiles(mv, 0, 2, rstd_kv_tok)
                token_tiles(mv, 1, 2, rstd_kv_tok)
                at_tile = 0
                for u in range(10):
                    split()
                    U.up()
                    while at_tile < 12 and 6 * (at_tile + 1) <= 8 * (u + 1):
                        join(qr[:, at_tile, :] if at_tile < 4 else mqk[:, 2 * (at_tile - 4), :])
                        at_tile += 1
                with loop(dve, HEADS // 2, (U, 16), (T, 8), (HD, 2), (STEP, 2 * DVE_HEAD_STEPS)) as i:
                    for e in range(2):
                        def gate_tile(m):
                            join(flat(gates[:, bass.ds(i * 8 + 4 * e + m, 1), :]))

                        halves(3)
                        dve.wait_ge(s_done, HD.at(1))
                        step(dve.scalar_tensor_tensor(out=prob[:, :], in0=p_ml[:, 0:384], scalar=MLA_SCALE,
                                                      in1=c_(MNEG, 384), op0=ALU.mult, op1=ALU.add))
                        dve.tensor_reduce(stat[:, 0:1], prob[:, 0:P], AX.X, ALU.max)
                        step(dve.tensor_reduce(stat[:, 1:2], prob[:, P:384], AX.X, ALU.max))
                        dve.tensor_scalar(stat[:, 2:4], stat[:, 0:2], -1.0, None, ALU.mult).then_inc(max_ready, 1)
                        halves(1)
                        dve.wait_ge(ln_done, HD.at(1))
                        step(dve.scalar_tensor_tensor(out=sp[:, :], in0=p_sb[:, 0:384], scalar=0.0, in1=sp[:, :],
                                                      op0=ALU.max, op1=ALU.add))
                        dve.tensor_tensor(sp[:, :], sp[:, :], c_(KEEP, 384), ALU.mult).then_inc(sp_ready, 1)
                        halves(1)
                        dve.wait_ge(exp_done, HD.at(1))
                        step(dve.reciprocal(stat[:, 4:6], stat[:, 4:6]))
                        dve.tensor_scalar(prob[:, 0:P], prob[:, 0:P], stat[:, 4:5], None, ALU.mult)
                        dve.tensor_scalar(prob[:, P:384], prob[:, P:384], stat[:, 5:6], None, ALU.mult).then_inc(prob_ready, 1)
                        halves(1)
                        split()
                        dve.wait_ge(p_done, HD.at(1))
                        dve.scalar_tensor_tensor(out=wgt[:, :], in0=p_sb[:, 0:384], scalar=0.0, in1=c_(SBNEG, 384),
                                                 op0=ALU.min, op1=ALU.add).then_inc(logw_ready, 1)
                        gate_tile(0)
                        gate_tile(1)
                        U.up()
                        split()
                        gate_tile(2)
                        gate_tile(3)
                        U.up()
                        for out, o_hi, done, free in ((osb, osb_hi, p_sb, osb_free), (omla, om_hi, p_ml, om_free)):
                            dve.wait_ge(o_hi, HD.at(1))
                            o = out[:, bass.ds(i * 2 + e, 1), :]
                            dve.tensor_tensor(flat(o[:, :, S:2 * S]), done[:, 0:S], flat(o[:, :, 0:S].bitcast(F32)),
                                              ALU.subtract).then_inc(free, 1)
                        HD.up()
                with loop(dve, 4, (U, 8), (T, 8), (G, 4), (STEP, 8)) as i:
                    halves(2)
                    four_tiles(lambda m: psb[:, m, :])
                    halves(2)

                    def mix(n):
                        for m in range(n, n + 2):
                            dve.wait_ge(sig_done, G.at(m + 1))
                            dve.wait_ge(tiles_free, T.at(m - n - 1 + TILE_CREDIT))
                            step(dve.tensor_tensor(pmla[:, m, :], pmla[:, m, :], sig[:, m, S:2 * S], ALU.mult))
                            dve.wait_ge(psb_gated, G.at(m + 1))
                            dve.tensor_tensor(pmla[:, m, :], pmla[:, m, :], psb[:, m, :], ALU.add).then_inc(mix_f32, 1)

                    def mix_lo(n):
                        for m in range(n, n + 2):
                            dve.wait_ge(mix_hi, G.at(m + 1))
                            b = blend[:, bass.ds(i * 4 + m, 1), :]
                            step(dve.tensor_tensor(flat(b[:, :, S:2 * S]), pmla[:, m, :],
                                                   flat(b[:, :, 0:S].bitcast(F32)), ALU.subtract))
                            dve.sem_inc(mix_ready, 1)

                    split()
                    join(pmla[:, 0, :])
                    join(pmla[:, 1, :])
                    U.up()
                    split()
                    mix(0)
                    join(pmla[:, 2, :])
                    join(pmla[:, 3, :])
                    mix_lo(0)
                    U.up()
                    mix(2)
                    mix_lo(2)
                    G.up(4)

                def residual_tiles(i, next_norm, nhalves=6, gain=None):
                    def pair(n):
                        for m in range(n, n + 2):
                            xt = flat(x[:, bass.ds(i * 4 + m, 1), :])
                            dve.wait_ge(tmp_ready, T.at(1))
                            step(dve.tensor_tensor(xt, xt, tmp[:, T.const % 2, :], ALU.add))
                            dve.tensor_tensor(xt, res[T.const % BANKS][:, 0:S], xt, ALU.add).then_inc(tiles_free, 1)
                            T.up()

                    def low(n):
                        for m in range(n, n + 2) if next_norm else ():
                            low_h(i * 4 + m, gain4[:, m:m + 1] if gain is None else norms[:, gain + 4 * i + m:gain + 4 * i + m + 1])

                    halves(nhalves)
                    split()
                    pair(0)
                    U.up()
                    split()
                    low(0)
                    pair(2)
                    U.up()
                    low(2)

                with loop(dve, 4, (U, 8), (T, 4), (STEP, 4), (X, 4)) as i:
                    residual_tiles(i, True)
                step(dve.memset(uconv[:, :, 0:2], 0.0))

                def conv(m, dst, taps):
                    dve.wait_ge(tap2_done, FT.at(1))
                    step(dve.scalar_tensor_tensor(out=dst[:, m, :], in0=uconv[:, m, 1:1 + S],
                                                  scalar=taps[:, 4 * m + 1:4 * m + 2], in1=dst[:, m, :],
                                                  op0=ALU.mult, op1=ALU.add))
                    dve.scalar_tensor_tensor(out=dst[:, m, :], in0=uconv[:, m, 0:S], scalar=taps[:, 4 * m:4 * m + 1],
                                             in1=dst[:, m, :], op0=ALU.mult, op1=ALU.add).then_inc(conv_done, 1)
                    FT.up()

                def product_lo(i, m):
                    dve.wait_ge(ffn_hi, FP.at(1))
                    b = blend[:, bass.ds(i * 4 + m, 1), :]
                    step(dve.tensor_tensor(flat(b[:, :, S:2 * S]), fgate[:, m, :], flat(b[:, :, 0:S].bitcast(F32)),
                                           ALU.subtract))
                    dve.sem_inc(ffn_ready, 1)
                    FP.up()

                def group_tiles(dst, taps):
                    split()
                    join(uconv[:, 0, 2:2 + S])
                    join(uconv[:, 1, 2:2 + S])
                    U.up()
                    split()
                    conv(0, dst, taps)
                    conv(1, dst, taps)
                    join(uconv[:, 2, 2:2 + S])
                    join(uconv[:, 3, 2:2 + S])
                    U.up()

                def gate_group(i, part_start):
                    if part_start:
                        halves(6)
                    else:
                        split()
                        product_lo(i - 1, 0)
                        product_lo(i - 1, 1)
                        U.up()
                        split()
                        product_lo(i - 1, 2)
                        product_lo(i - 1, 3)
                        U.up()
                        halves(4)
                    group_tiles(fgate, taps_g)

                def value_group():
                    split()
                    conv(2, fgate, taps_g)
                    conv(3, fgate, taps_g)
                    U.up()
                    halves(5)
                    group_tiles(fval, taps_v)
                    conv(2, fval, taps_v)
                    conv(3, fval, taps_v)

                for groups in PARTS:
                    gate_group(0, True)
                    with loop(dve, groups - 1, (U, 16), (T, 8), (FT, 8), (FP, 4), (STEP, 12)) as i:
                        value_group()
                        gate_group(i + 1, False)
                    value_group()
                    for m in range(4):
                        product_lo(groups - 1, m)
                    if groups == 4:
                        with loop(dve, 4, (U, 8), (T, 4), (STEP, 4)) as i:
                            residual_tiles(i, False)
                    else:
                        for i in range(4):
                            residual_tiles(i, True, 4, N1)
                N.up(SUMS)
            dve.wait_ge(rstd_ready, N.at(1) + ONE_UP)
            for q in range(4):
                for k in range(4 * q, 4 * q + 4):
                    ins = dve.scalar_tensor_tensor(out=x[:, k, :], in0=x[:, k, :],
                                                   scalar=par[:, L * PCOLS + k:L * PCOLS + k + 1], in1=rstd[:, :],
                                                   op0=ALU.mult, op1=ALU.mult)
                ins.then_inc(x_done, 1)

        @block.gpsimd
        def _(pool):
            SQ, N, HD, G, STEP, T, W, FP = (Count() for _ in range(8))
            pool.sem_inc(scaled, ONE_UP)

            def flat(t):
                return t.rearrange("p a t -> p (a t)")

            def step(ins):
                ins.then_inc(pool_step, 1)
                STEP.up()
                pool.wait_ge(pool_step, STEP.at())

            def scale(t, factor, last=1):
                pool.wait_ge(tiles_free, T.at(1 + TILE_CREDIT))
                pool.tensor_tensor(t, t, factor[:, :], ALU.mult).then_inc(scaled, 1)
                T.up(last)
                W.up()

            def add_squares(n, fresh=True):
                if fresh:
                    pool.wait_ge(sum_done, N.at() + ONE_UP)
                    N.up()
                    pool.wait_ge(sq_ready, SQ.at(2))
                    pool.tensor_tensor(sqsum[:, :], sq[:, 0, :], sq[:, 1, :], ALU.add).then_inc(sq_added, 2)
                    SQ.up(2)
                    n -= 2
                for _ in range(n):
                    pool.wait_ge(sq_ready, SQ.at(1))
                    pool.wait_ge(sq_added, SQ.at())
                    pool.tensor_tensor(sqsum[:, :], sqsum[:, :], sq[:, SQ.const % 2, :], ALU.add).then_inc(sq_added, 1)
                    SQ.up()

            def rotate(t):
                pool.wait_ge(scaled, W.at() + ONE_UP)
                for q in range(0, P, 32):
                    o = q ^ 32
                    step(pool.tensor_tensor(swap[q:q + 32, :], t[o:o + 32, :], cst[o:o + 32, SIN:SIN + S], ALU.mult))
                step(pool.tensor_tensor(t, t, c_(COS, S), ALU.mult))
                pool.tensor_tensor(t, t, swap[:, :], ALU.add).then_inc(rope_done, 1)

            SQ.up(DT)
            N.up()
            pool.wait_ge(cst_in, 16)
            with loop(pool, L, (SQ, SQUARES), (N, SUMS), (HD, HEADS), (G, DT), (STEP, POOL_STEPS), (T, TILES),
                      (W, SCALED), (FP, FF // P)) as l:
                pool.wait_ge(rstd_ready, N.at() + ONE_UP)
                for m in range(4):
                    scale(sbqk[:, m, :], rstd)
                with loop(pool, 3, (T, 4), (W, 4)) as i:
                    for m in range(4):
                        scale(flat(sbqk[:, bass.ds(i * 4 + (4 + m), 1), :]), rstd)
                T.up(4)
                for k in range(CKVT):
                    scale(craw[:, k, :], rstd)
                add_squares(4)
                for k in range(4):
                    scale(craw[:, CKVT + k, :], rstd)
                add_squares(4)
                for k in range(2):
                    scale(craw[:, CKVT + 4 + k, :], rstd)
                scale(kr[:, :], rstd, 2)
                add_squares(2, fresh=False)
                pool.wait_ge(sq_added, SQ.at())
                rotate(kr[:, :])
                pool.wait_ge(rstd_ready, N.at(-1) + ONE_UP)
                for m in range(HEADS):
                    scale(mqk[:, 2 * m + 1, :], rstd_kv)
                T.up(4)
                pool.wait_ge(rstd_ready, N.at() + ONE_UP)
                pool.wait_ge(rope_done, l * 5 + 1)
                for p in range(HEADS // 2):
                    scale(qr[:, p, :], rstd_q)
                    rotate(qr[:, p, :])
                    pool.wait_ge(rope_done, l * 5 + (p + 2))
                for m in range(HEADS):
                    scale(mqk[:, 2 * m, :], rstd_q)
                with loop(pool, HEADS // 2, (HD, 2), (T, 8), (W, 8)) as i:
                    for e in range(2):
                        def head_cols(t, b):
                            return t[:, b, bass.ds(i * (2 * P) + e * P, P)]

                        pool.wait_ge(om_done, HD.at() + ONE_UP)
                        pool.wait_ge(scaled, W.at() + ONE_UP)
                        pool.tensor_copy(qn_st[:, :], flat(mqk[:, bass.ds(i * 4 + 2 * e, 1), :]))
                        if e == 0:
                            pool.tensor_copy(qr_st[:, :], flat(qr[:, bass.ds(i, 1), :]))
                        for b in range(2):
                            pool.tensor_copy(v_st[:, b, :], head_cols(v, b))
                            ins = pool.tensor_copy(mv_st[:, b, :], head_cols(mv, b))
                        ins.then_inc(staged, 1)
                        HD.up()
                        for m in range(4):
                            scale(flat(gates[:, bass.ds(i * 8 + (4 * e + m), 1), :]), rstd)
                with loop(pool, 4, (G, 4), (T, 8)):
                    for m in range(4):
                        pool.wait_ge(sig_done, G.at(1))
                        pool.wait_ge(tiles_free, T.at(m + 1 + TILE_CREDIT))
                        pool.tensor_tensor(psb[:, m, :], psb[:, m, :], sig[:, m, 0:S], ALU.mult).then_inc(psb_gated, 1)
                        G.up()
                    T.up(8)
                T.up(DT)
                add_squares(DT)
                pool.wait_ge(rstd_ready, N.at() + ONE_UP)

                def group():
                    for m in range(4):
                        scale(uconv[:, m, 2:2 + S], rstd)

                def products():
                    for m in range(4):
                        pool.wait_ge(silu_done, FP.at(1))
                        pool.wait_ge(conv_done, FP.at(0, 4, 8, 4 + m + 1 + ONE_UP))
                        pool.tensor_tensor(fgate[:, m, :], fgate[:, m, :], fval[:, m, :], ALU.mult).then_inc(ffn_f32, 1)
                        FP.up()

                for groups in PARTS:
                    group()
                    with loop(pool, groups - 1, (T, 8), (W, 8), (FP, 4)):
                        group()
                        products()
                        group()
                    group()
                    products()
                    T.up(DT)
                add_squares(DT)


ACT_STEPS = 3 + 1 + 2 * HEADS + 4 + 4
DVE_HEAD_STEPS = 4
DVE_STEPS = HEADS * DVE_HEAD_STEPS + 2 * DT + DT + 1 + 2 * FF // P + FF // P + 3 * DT
POOL_STEPS = 5 * 5


def stat_seed(cst):
    return cst[:, ONE:ONE + 1]


def _tiles(w):
    k, m = w.shape
    return w.reshape(k // P, P, m // P, P).transpose(0, 2, 1, 3)


def _blocked(w, kb=4, nm=4):
    t = _tiles(w)
    out = []
    for m0 in range(0, t.shape[1], nm):
        for k0 in range(0, t.shape[0], kb):
            out.append(t[k0:k0 + kb, m0:m0 + nm].transpose(1, 0, 2, 3).reshape(-1, P, P))
    return np.concatenate(out)


def _rows(w):
    t = _tiles(w)
    return np.concatenate([t[:, m:m + 4].reshape(-1, P, P) for m in range(0, t.shape[1], 4)])


def _layer_stream(w_in, w_uq, w_ukv, w_psb, w_pmla, w_out, w_up, w_down):
    cut = np.cumsum([0, 1024, 1024, 1024, CQ, CKV, ROPE, D, D])
    q, k, v, cq, ckv, kr, gs, gm = (w_in[:, a:b] for a, b in zip(cut[:-1], cut[1:]))
    pair = lambda a, b: np.stack([a.reshape(len(a), -1, P), b.reshape(len(b), -1, P)], 2).reshape(len(a), -1)
    uq = w_uq.reshape(CQ, HEADS, P + ROPE)
    ukv = w_ukv.reshape(CKV, HEADS, 2, P)
    parts = [
        _blocked(pair(q, k)), _rows(v), _blocked(ckv), _blocked(cq[:, :512]),
        _blocked(np.concatenate([cq[:, 512:], kr, kr], 1), 4, 3),
        _blocked(ukv[:, :, 0].reshape(CKV, -1)), _rows(ukv[:, :, 1].reshape(CKV, -1)),
        _blocked(uq[:, :, P:].reshape(CQ, -1), CQT, 4), _blocked(uq[:, :, :P].reshape(CQ, -1), CQT, 8),
        np.zeros((8, P, P), w_in.dtype),
        _blocked(pair(gs, gm)),
    ]
    a, b = _blocked(w_psb), _blocked(w_pmla)
    for g in range(4):
        parts += [a[32 * g:32 * g + 32], b[32 * g:32 * g + 32]]
    parts.append(_blocked(w_out))
    g0 = 0
    for n in PARTS:
        for g in range(g0, g0 + n):
            parts += [_blocked(w_up[:, 512 * g:512 * g + 512]), _blocked(w_up[:, FF + 512 * g:FF + 512 * g + 512])]
        parts.append(_blocked(w_down[512 * g0:512 * (g0 + n)]))
        g0 += n
    t = np.concatenate(parts)
    assert len(t) == 8 * HALVES, len(t)
    return t.reshape(HALVES // 2, 16, P, P).transpose(0, 2, 1, 3)


def _consts():
    c = np.zeros((P, CCOLS), np.float32)
    inv = 1.0 / (np.float32(10000.0) ** (np.arange(0, ROPE, 2, dtype=np.float32) / np.float32(ROPE)))
    ang = np.arange(S, dtype=np.float32)[:, None] * inv[None, :].astype(np.float32)
    c[:, COS:COS + S] = np.tile(np.cos(ang).T, (4, 1))
    c[:, SIN:SIN + S] = np.tile(np.concatenate([np.sin(ang).T, -np.sin(ang).T]), (2, 1))
    p, f = np.arange(P)[:, None], np.arange(P)[None, :]
    keep = (p < f).astype(np.float32)
    seen = f // 64 <= p // 64
    for b in (0, 2):
        c[:, KEEP + b * P:KEEP + b * P + P] = keep
        c[:, SBNEG + b * P:SBNEG + b * P + P] = np.where(keep > 0, 0, MASKED)
        c[:, MNEG + b * P:MNEG + b * P + P] = np.where(seen, 0, MASKED)
    c[:, KEEP + P:KEEP + 2 * P] = 1
    c[:, TRI:TRI + P] = np.where(p >= f, -1, 0)
    c[:, NEG:NEG + P] = -1
    c[:, ONE:ONE + P] = 1
    c[:, EYE:EYE + P] = np.eye(P)
    return c


def kernel(x, norm1_g, w_in, b_gate, q_norm_g, w_uq, kv_norm_g, w_ukv, w_proj_sb, w_proj_mla, w_out,
           norm2_g, w_up, conv_w, conv_b, w_down, final_g):
    import concourse.bacc as bacc
    from concourse.bass_utils import run_bass_kernel_spmd

    a = [np.asarray(t) for t in (w_in, w_uq, w_ukv, w_proj_sb, w_proj_mla, w_out, w_up, w_down)]
    stream = np.zeros((CHUNKS + 2, P, 16, P), a[0].dtype)
    for l in range(L):
        stream[l * HALVES // 2:(l + 1) * HALVES // 2] = _layer_stream(*(t[l] for t in a))

    def cols(t):
        return np.asarray(t).reshape(-1, P).T

    par = []
    for l in range(L):
        bg = np.asarray(b_gate[l]).reshape(2, DT, P).transpose(2, 1, 0).reshape(P, 2 * DT)
        taps = np.concatenate([np.asarray(conv_w[l]), np.asarray(conv_b[l])[None]])
        taps = taps.reshape(4, 2, sum(PARTS), 4, P).transpose(4, 2, 1, 3, 0).reshape(P, -1)
        par += [cols(norm1_g[l]), cols(norm2_g[l]), cols(kv_norm_g[l]), cols(q_norm_g[l]), bg, taps]
    par = np.ascontiguousarray(np.concatenate(par + [cols(final_g)], 1))
    xt = np.ascontiguousarray(np.asarray(x)[0].T.reshape(DT, P, S).transpose(1, 0, 2))

    nc = bacc.Bacc("TRN2", target_bir_lowering=False, num_devices=1)
    ins = {"x_t": xt, "stream": stream, "par_in": par, "cst_in": _consts()}
    args = [nc.dram_tensor(n, t.shape, F32, kind="ExternalInput").ap() for n, t in ins.items()]
    y = nc.dram_tensor("y_t", (P, DT, S), F32, kind="ExternalOutput").ap()
    trunk(nc, *args, y)
    r = run_bass_kernel_spmd(nc, [ins], core_ids=[0])
    got = r.results[0]["y_t"]
    return np.ascontiguousarray(got.transpose(1, 0, 2).reshape(D, S).T[None])
```

```python
from contextlib import ExitStack, contextmanager

import numpy as np

import concourse.bass as bass
from concourse import mybir

F32 = mybir.dt.float32
F32R = mybir.dt.float32r
ALU = mybir.AluOpType
ACT = mybir.ActivationFunctionType
AX = mybir.AxisListType

P = 128
L = 2
D = 2048
S = 256
DT = D // P
HEADS = 8
ROPE = 64
CQ, CKV = 768, 512
CQT, CKVT = CQ // P, CKV // P
FF = 5632
EPS = 1e-6
SB_SCALE = float(P) ** -0.5
MLA_SCALE = float(P + ROPE) ** -0.5
MASKED = -1e38

PARTS = (4, 4, 3)

RAW = 4
HIS = 4
AHEAD = 3
BANKS = 4
HALVES = 480
TILES = 272
CHUNKS = L * HALVES // 2
FIRST_HALVES = ((0, 1), (2,), (), ())
HALF_CREDIT = 8
TILE_CREDIT = 4
ACT_CREDIT = 4
ONE_UP = 1

N1, N2, CG, BG, CONV = 0, 16, 32, 42, 74
PCOLS = CONV + 32 * sum(PARTS)
COS, SIN, KEEP, SBNEG, MNEG, TRI, NEG, ONE, EYE = 0, 256, 512, 768, 1152, 1536, 1664, 1792, 1920
CCOLS = 2048


class Count:

    def __init__(self):
        self.const, self.terms = 0, []

    def at(self, k=0, div=1, mul=1, plus=0):
        v = ((self.const + k) // div) * mul + plus
        for reg, per in self.terms:
            assert per % div == 0
            v = reg * (per // div * mul) + v
        return v

    def up(self, n=1):
        self.const += n


@contextmanager
def loop(eng, trips, *counts):
    with eng.Fori(0, trips) as i:
        began = [c.const for c, _ in counts]
        for c, per in counts:
            c.terms.append((i, per))
        yield i
        for (c, per), b in zip(counts, began):
            assert c.const - b == per, (c.const - b, per)
            c.terms.pop()
            c.const = b + trips * per


def blocked(nk, nm, kb=4):
    return [(m, k) for b in range(0, nk, kb) for m in range(nm) for k in range(b, b + kb)]


def trunk(nc, x_in, stream, params, consts, y_out):
    ctx = ExitStack()
    with ctx:
        top = [16384]

        def at(name, shape, dt, offset):
            return nc.alloc_sbuf_tensor_at(name, shape, dt, offset=offset)

        def new(name, shape, dt=F32):
            o = top[0]
            size = 4 * int(np.prod(shape[1:]))
            top[0] = o + (size + 31) // 32 * 32
            return at(name, shape, dt, o), o

        x, _ = new("x", [P, DT, S])
        h, _ = new("h", [P, DT, 2 * S], F32R)
        raw, o = new("raw", [P, RAW, 16, P])
        lo = at("lo", [P, RAW, 16, P], F32R, o)
        hi, _ = new("hi", [P, HIS, 8, P], F32R)
        blend, r1 = new("blend", [P, 16, 2 * S], F32R)
        gates = at("gates", [P, 32, S], F32, r1)
        craw = at("craw", [P, CKVT + CQT, S], F32, r1)
        chl = at("chl", [P, CKVT + CQT, 2 * S], F32R, r1 + 4 * (CKVT + CQT) * S)
        sbqk, r2 = new("sbqk", [P, 16, S])
        osb = at("osb", [P, HEADS, 2 * S], F32R, r2)
        xsq = at("xsq", [P, DT, S], F32, r2)
        uconv = at("uconv", [P, 4, S + 8], F32, r2)
        fgate = at("fgate", [P, 4, S], F32, r2 + 4 * 4 * (S + 8))
        fval = at("fval", [P, 4, S], F32, r2 + 4 * 4 * (S + 8) + 4 * 4 * S)
        v, r3 = new("v", [P, 2, 1024])
        sig = at("sig", [P, 4, 2 * S], F32, r3)
        mqk, r4 = new("mqk", [P, 16, S])
        omla = at("omla", [P, HEADS, 2 * S], F32R, r4)
        qr, _ = new("qr", [P, HEADS // 2, S])
        kr, _ = new("kr", [P, S])
        mv, r5 = new("mv", [P, 2, 1024])
        psb = at("psb", [P, 4, S], F32, r5)
        pmla = at("pmla", [P, 4, S], F32, r5 + 4 * 4 * S)

        k_st, _ = new("k_st", [P, S])
        v_st, _ = new("v_st", [P, 2, P])
        qn_st, o = new("qn_st", [P, S])
        swap = at("swap", [P, S], F32, o)
        qr_st, _ = new("qr_st", [P, S])
        mv_st, _ = new("mv_st", [P, 2, P])
        tmp, _ = new("tmp", [P, 2, S])
        sp, o = new("sp", [P, 384])
        sp_lo = at("sp_lo", [P, 384], F32R, o)
        rstd_kv = at("rstd_kv", [P, S + 2], F32, o)
        wgt, o = new("wgt", [P, 384])
        sp_hi = at("sp_hi", [P, 384], F32R, o)
        sqsum = at("sqsum", [P, S], F32, o)
        prob, o = new("prob", [P, 384])
        probT, _ = new("probT", [P, 384])
        sq = at("sq", [P, 2, S], F32, o)
        rstd, _ = new("rstd", [P, S + 2])
        rstd_q, _ = new("rstd_q", [P, 2])
        cst, _ = new("cst", [P, CCOLS])
        suffix, _ = new("suffix", [P, 2 * P], F32R)
        par, _ = new("par", [P, L * PCOLS + DT])
        norms, _ = new("norms", [P, BG])
        bias8, _ = new("bias8", [P, 8])
        gain4, _ = new("gain4", [P, 4])
        taps_g, _ = new("taps_g", [P, 16])
        taps_v, _ = new("taps_v", [P, 16])
        stat, _ = new("stat", [P, 8])
        assert top[0] <= 229344, top[0]

        def c_(a, n=P):
            return cst[:, a:a + n]

        def bank(name):
            return ctx.enter_context(nc.psum_tensor(name, [P, 512], F32))

        res = [bank(f"res{b}") for b in range(BANKS)]
        p_sb, p_ml, p_tr, p_st = bank("p_sb"), bank("p_ml"), bank("p_tr"), bank("p_st")

        def sem(name):
            return ctx.enter_context(nc.semaphore(name))

        landed = [sem(f"landed{s}") for s in range(RAW)]
        hi_done = sem("hi_done")
        split_done = sem("split_done")
        halves_used = sem("halves_used")
        tiles_done = sem("tiles_done")
        tmp_ready = sem("tmp_ready")
        tiles_free = sem("tiles_free")
        first_half_in = sem("first_half_in")
        gain1_in, par_in, cst_in, y_out_sem = sem("gain1_in"), sem("par_in"), sem("cst_in"), sem("y_out_sem")
        x_landed = [sem(f"x_landed{q}") for q in range(4)]
        x_done = sem("x_done")
        y_gained, y_done = sem("y_gained"), sem("y_done")
        dve_step, act_step, pool_step = sem("dve_step"), sem("act_step"), sem("pool_step")
        sq_ready = sem("sq_ready")
        sq_added = sem("sq_added")
        sum_done = sem("sum_done")
        rstd_ready = sem("rstd_ready")
        root_ready = sem("root_ready")
        scaled = sem("scaled")
        h_hi = sem("h_hi")
        h_ready = sem("h_ready")
        c_hi, c_ready = sem("c_hi"), sem("c_ready")
        gain_in = sem("gain_in")
        rope_done = sem("rope_done")
        taps_in = sem("taps_in")
        k_staged, staged = sem("k_staged"), sem("staged")
        z_done, ln_done, p_done = sem("z_done"), sem("ln_done"), sem("p_done")
        sp_f32, sp_hi_done, sp_ready = sem("sp_f32"), sem("sp_hi_done"), sem("sp_ready")
        logw_ready, w_ready, osb_done = sem("logw_ready"), sem("w_ready"), sem("osb_done")
        osb_hi, osb_free = sem("osb_hi"), sem("osb_free")
        s_done, max_ready, exp_done, prob_ready = sem("s_done"), sem("max_ready"), sem("exp_done"), sem("prob_ready")
        tr_done, tr_copied, om_done = sem("tr_done"), sem("tr_copied"), sem("om_done")
        om_hi, om_free = sem("om_hi"), sem("om_free")
        sig_done, psb_gated, mix_f32, mix_hi, mix_ready = (
            sem("sig_done"), sem("psb_gated"), sem("mix_f32"), sem("mix_hi"), sem("mix_ready"))
        tap2_done, conv_done, silu_done, ffn_f32, ffn_hi, ffn_ready = (
            sem("tap2_done"), sem("conv_done"), sem("silu_done"), sem("ffn_f32"), sem("ffn_hi"), sem("ffn_ready"))

        SCALED = 16 + 11 + HEADS + 2 * DT + 2 * (FF // P)
        SUMS = 4
        SQUARES = CKVT + CQT + 2 * DT

        block = ctx.enter_context(nc.Block())

        @block.sync
        def _(sp_):
            sp_.dma_start(par[:, 0:DT], params[:, 0:DT]).then_inc(gain1_in, 16)
            for s in range(RAW):
                for q in ((0,), (1,), (2, 3), ())[s]:
                    sp_.dma_start(x[:, 4 * q:4 * q + 4, :], x_in[:, 4 * q:4 * q + 4, :]).then_inc(x_landed[q], 16)
                if s == 0:
                    sp_.dma_start(raw[:, 0, 0:8, :], stream[0, :, 0:8, :]).then_inc(first_half_in, 16)
                    sp_.dma_start(raw[:, 0, 8:16, :], stream[0, :, 8:16, :]).then_inc(landed[0], 16)
                else:
                    sp_.dma_start(raw[:, s, :, :], stream[s]).then_inc(landed[s], 16)
            sp_.dma_start(cst[:, :], consts).then_inc(cst_in, 16)
            sp_.dma_start(par[:, DT:], params[:, DT:]).then_inc(par_in, 16)
            with sp_.Fori(0, CHUNKS // RAW - 1) as i:
                for s in range(RAW):
                    sp_.wait_ge(halves_used, i * (2 * RAW) + (2 * s + 3 + HALF_CREDIT))
                    sp_.dma_start(raw[:, s, :, :], stream[i * RAW + (RAW + s)]).then_inc(landed[s], 16)
            for s in range(2):
                sp_.wait_ge(halves_used, 2 * (CHUNKS + s) - 2 * RAW + 3 + HALF_CREDIT)
                sp_.dma_start(raw[:, s, :, :], stream[CHUNKS + s]).then_inc(landed[s], 16)
            for q, ready, number in ((0, x_done, 1), (3, y_done, 1), (1, x_done, 2), (2, x_done, 3)):
                sp_.wait_ge(ready, number)
                sp_.dma_start(y_out[:, 4 * q:4 * q + 4, :], x[:, 4 * q:4 * q + 4, :]).then_inc(y_out_sem, 16)
            sp_.wait_ge(y_out_sem, 64)
            sp_.wait_ge(first_half_in, 16)
            for s in range(RAW):
                sp_.wait_ge(landed[s], 16 * (CHUNKS // RAW + (s < 2)))

        @block.tensor
        def _(pe):
            U, T, HD = Count(), Count(), Count()
            pe.sem_inc(halves_used, HALF_CREDIT)
            for started in (z_done, om_done, sum_done):
                pe.sem_inc(started, ONE_UP)

            def half_ready():
                pe.wait_ge(split_done, U.at(1))

            def w_tile(idx):
                u = U.const
                return hi[:, u % HIS, idx, :], lo[:, u // 2 % RAW, 8 * (u % 2) + idx, :]

            def gemm(seq, nk, moving, ready=None, last_tile_inc=1, last_half_inc=1):
                for s, (m, k) in enumerate(seq):
                    idx = s % 8
                    if idx == 0:
                        half_ready()
                    if k == 0:
                        pe.wait_ge(tiles_free, T.at(m + 1))
                    if ready and k % 4 == 0 and m == seq[0][0]:
                        ready(k)
                    out = res[(T.const + m) % BANKS]
                    w_hi, w_lo = w_tile(idx)
                    end = s == len(seq) - 1
                    a = pe.matmul(out[:, :], w_hi, moving(k), start=(k == 0), stop=(k == nk - 1), skip_group_check=True)
                    b = pe.matmul(out[:, 0:S], w_lo, moving(k)[:, 0:S], start=False, stop=(k == nk - 1), skip_group_check=True)
                    if idx == 7 or end:
                        a.then_inc(halves_used, last_half_inc if end else 1)
                        U.up(last_half_inc if end else 1)
                    if k == nk - 1:
                        b.then_inc(tiles_done, last_tile_inc if end else 1)

            def gemm_tokens(nk, acts, ready=None):
                for kp in range(nk // 2):
                    half_ready()
                    if ready and kp % 2 == 0:
                        ready(2 * kp)
                    for blk in range(2):
                        out = res[(T.const + blk) % BANKS]
                        if kp == 0:
                            pe.wait_ge(tiles_free, T.at(blk + 1))
                        for j in range(2):
                            k = 2 * kp + j
                            u = U.const
                            w_hi = hi[:, u % HIS, 4 * j:4 * j + 4, :]
                            w_lo = lo[:, u // 2 % RAW, 8 * (u % 2) + 4 * j:8 * (u % 2) + 4 * j + 4, :]
                            a_hi = acts(k)[:, blk * P:blk * P + P]
                            a_lo = acts(k)[:, S + blk * P:S + blk * P + P]
                            pe.matmul(out[:, :], a_hi, w_hi, start=(k == 0), stop=False, skip_group_check=True)
                            a = pe.matmul(out[:, :], a_lo, w_hi, start=False, stop=False, skip_group_check=True)
                            b = pe.matmul(out[:, :], a_hi, w_lo, start=False, stop=(k == nk - 1), skip_group_check=True)
                            if blk == 1 and j == 1:
                                a.then_inc(halves_used, 1)
                            if k == nk - 1:
                                b.then_inc(tiles_done, 1)
                    U.up()
                T.up(2)

            def norm_sum(number, squares, tokens=False, features=True):
                pe.wait_ge(sq_added, squares)
                pe.wait_ge(rstd_ready, number + ONE_UP)
                if tokens:
                    for b in range(2):
                        done = pe.matmul(p_st[:, S + b:S + b + 1], sqsum[:, b * P:b * P + P], c_(ONE, 1),
                                         start=(b == 0), stop=True, skip_group_check=True)
                if features:
                    done = pe.matmul(p_st[:, 0:S], c_(ONE), sqsum[:, :], start=not tokens, stop=True,
                                     skip_group_check=True)
                done.then_inc(sum_done, 1)

            def H(k):
                return h[:, k, :]

            def C(k):
                return chl[:, k, :]

            def B(k):
                return blend[:, k, :]

            def attention_scores(i, e):
                pe.wait_ge(k_staged, HD.at(1))
                pe.wait_ge(osb_free, HD.at() + ONE_UP)
                q = sbqk[:, bass.ds(i * 4 + 2 * e, 1), :].rearrange("p a t -> p (a t)")
                pe.matmul(p_sb[:, 0:S], k_st[:, 0:P], q, start=True, stop=True, skip_group_check=True)
                pe.matmul(p_sb[:, S:384], k_st[:, P:S], q[:, P:S], start=False, stop=True,
                          skip_group_check=True).then_inc(z_done, 1)
                pe.wait_ge(staged, HD.at(1))
                pe.wait_ge(om_free, HD.at() + ONE_UP)
                kn = mqk[:, bass.ds(i * 4 + 2 * e + 1, 1), :].rearrange("p a t -> p (a t)")
                r = slice(64 * e, 64 * e + 64)
                pe.matmul(p_ml[:, 0:P], qn_st[:, 0:P], kn[:, 0:P], start=True, stop=False, skip_group_check=True)
                pe.matmul(p_ml[:, 0:P], qr_st[r, 0:P], kr[r, 0:P], start=False, stop=True, skip_group_check=True)
                pe.matmul(p_ml[:, P:384], qn_st[:, P:S], kn, start=False, stop=False, skip_group_check=True)
                pe.matmul(p_ml[:, P:384], qr_st[r, P:S], kr[r, :], start=False, stop=True,
                          skip_group_check=True).then_inc(s_done, 1)

            def attention_weights():
                pe.wait_ge(sp_ready, HD.at(1))
                tri, neg = suffix[:, 0:P], suffix[:, P:2 * P]
                for part in (sp_hi, sp_lo):
                    pe.matmul(p_sb[:, 0:S], tri, part[:, 0:S], start=False, stop=True, skip_group_check=True)
                    pe.matmul(p_sb[:, P:S], neg, part[:, S:384], start=False, stop=True, skip_group_check=True)
                    last = pe.matmul(p_sb[:, S:384], tri, part[:, S:384], start=False, stop=True, skip_group_check=True)
                last.then_inc(p_done, 1)
                pe.wait_ge(prob_ready, HD.at(1))
                for b in range(3):
                    t = pe.transpose(p_tr[:, b * P:b * P + P], prob[:, b * P:b * P + P], c_(EYE))
                t.then_inc(tr_done, 1)

            def attention_values():
                pe.wait_ge(w_ready, HD.at(1))
                pe.matmul(p_sb[:, 0:S], v_st[:, 0, :], wgt[:, 0:S], start=True, stop=True, skip_group_check=True)
                pe.matmul(p_sb[:, P:S], v_st[:, 1, :], wgt[:, S:384], start=False, stop=True,
                          skip_group_check=True).then_inc(osb_done, 1)
                pe.wait_ge(tr_copied, HD.at(1))
                pe.matmul(p_ml[:, 0:S], mv_st[:, 0, :], probT[:, 0:S], start=True, stop=True, skip_group_check=True)
                pe.matmul(p_ml[:, P:S], mv_st[:, 1, :], probT[:, S:384], start=False, stop=True,
                          skip_group_check=True).then_inc(om_done, 1)
                HD.up()

            four = blocked(16, 4)
            with loop(pe, L, (U, HALVES), (T, TILES), (HD, HEADS)) as l:
                def first_h(k):
                    pe.wait_ge(h_ready, l * (2 * DT) + (k + 4))

                def second_h(k):
                    pe.wait_ge(h_ready, l * (2 * DT) + (DT + k + 4))

                gemm(four[:48], 16, H, first_h)
                pe.wait_ge(cst_in, 16)
                norm_sum(l * SUMS, l * SQUARES + DT, tokens=True)
                gemm(four[48:], 16, H, lambda k: first_h(12))
                T.up(4)
                with loop(pe, 3, (U, 8), (T, 4)):
                    gemm(four, 16, H)
                    T.up(4)
                for _ in range(2):
                    gemm_tokens(16, H)
                gemm(four, 16, H)
                T.up(4)
                gemm(four[:32], 16, H)
                norm_sum(l * SUMS + 1, l * SQUARES + DT + CKVT, tokens=True)
                gemm(four[32:], 16, H)
                T.up(4)
                gemm(blocked(16, 3), 16, H, last_tile_inc=2)
                T.up(4)
                pe.wait_ge(c_ready, l * 3 + 1)
                for _ in range(2):
                    gemm(blocked(4, 4), 4, C)
                    T.up(4)
                gemm_tokens(4, C)
                norm_sum(l * SUMS + 2, l * SQUARES + DT + CKVT + CQT, tokens=True, features=False)
                gemm_tokens(4, C)
                pe.wait_ge(c_ready, l * 3 + 3)
                gemm(blocked(CQT, 12, CQT), CQT, lambda k: C(CKVT + k), last_half_inc=2)
                T.up(12)
                with loop(pe, HEADS // 2, (U, 16), (T, 8), (HD, 2)) as i:
                    for e in range(2):
                        gemm(four[:16], 16, H)
                        attention_scores(i, e)
                        gemm(four[16:48], 16, H)
                        attention_weights()
                        gemm(four[48:], 16, H)
                        attention_values()
                        T.up(4)
                with loop(pe, 4, (U, 8), (T, 8)):
                    pe.wait_ge(osb_free, l * HEADS + HEADS + ONE_UP)
                    gemm(blocked(8, 4), 8, lambda k: osb[:, k, :])
                    T.up(4)
                    pe.wait_ge(om_free, l * HEADS + HEADS + ONE_UP)
                    gemm(blocked(8, 4), 8, lambda k: omla[:, k, :])
                    T.up(4)
                with loop(pe, 4, (U, 8), (T, 4)):
                    gemm(four, 16, B, lambda k: pe.wait_ge(mix_ready, l * DT + (k + 4)))
                    T.up(4)
                done = 0
                for part, groups in enumerate(PARTS):
                    if part == 0:
                        gemm(four[:48], 16, H, second_h)
                        norm_sum(l * SUMS + 3, l * SQUARES + DT + CKVT + CQT + DT)
                        gemm(four[48:], 16, H, lambda k: second_h(12))
                    else:
                        gemm(four, 16, H)
                    T.up(4)
                    with loop(pe, groups - 1, (U, 16), (T, 8)):
                        for _ in range(2):
                            gemm(four, 16, H)
                            T.up(4)
                    gemm(four, 16, H)
                    T.up(4)

                    def ffn_in(k, done=done):
                        pe.wait_ge(ffn_ready, l * (FF // P) + (done + k + 4 + ACT_CREDIT))

                    nk = 4 * groups
                    if nk == 16:
                        with loop(pe, 4, (U, 8), (T, 4)):
                            gemm(four, 16, B, ffn_in)
                            T.up(4)
                    else:
                        for _ in range(4):
                            gemm(blocked(nk, 4), nk, B, ffn_in)
                            T.up(4)
                    done += nk
            norm_sum(L * SUMS, L * SQUARES + DT)

        @block.scalar
        def _(act):
            U, T, HD, N, G, FT, FP, SQ, W, X = (Count() for _ in range(10))

            def split(k=AHEAD):
                u = U.const + k
                if k == 0:
                    act.wait_ge(first_half_in, 16)
                elif k == 1:
                    act.wait_ge(landed[0], 16)
                elif u % 2 == 0:
                    act.wait_ge(landed[u // 2 % RAW], U.at(k, 8, 16, 16))
                act.wait_ge(halves_used, U.at(k + 1 - HIS + HALF_CREDIT))
                act.activation(hi[:, u % HIS, :, :], raw[:, u // 2 % RAW, 8 * (u % 2):8 * (u % 2) + 8, :],
                               ACT.Copy).then_inc(hi_done, 1)

            def halves(n):
                for _ in range(n):
                    split()
                    U.up()

            def take(last=1):
                act.wait_ge(tiles_done, T.at(1))
                act.wait_ge(tiles_free, T.at(3))
                act.activation(tmp[:, T.const % 2, :], res[T.const % BANKS][:, S:2 * S], ACT.Copy).then_inc(tmp_ready, last)
                T.up(last)

            def root(n, dst, src, factor=1.0):
                act.wait_ge(sum_done, N.at(1) + ONE_UP)
                act.activation(dst, src, ACT.Sqrt, scale=1.0 / (n * factor ** 2),
                               bias=EPS / factor ** 2).then_inc(root_ready, 1)
                N.up()

            def square(src):
                act.wait_ge(sq_added, SQ.at(-1))
                act.activation(sq[:, SQ.const % 2, :], src, ACT.Square).then_inc(sq_ready, 1)
                SQ.up()

            def flat(t):
                return t.rearrange("p a t -> p (a t)")

            def load_table(func):
                act.activation(stat[:, 6:7], par[:, 0:1], func, scale=0.0, bias=1.0)

            STEP = Count()
            act.sem_inc(sq_ready, DT)
            SQ.up(DT)
            act.wait_ge(gain1_in, 16)
            load_table(ACT.Sqrt)
            for q in range(4):
                act.wait_ge(x_landed[q], 16)
                for k in range(4 * q, 4 * q + 4):
                    act.activation(h[:, k, 0:S], x[:, k, :], ACT.Copy, scale=par[:, N1 + k:N1 + k + 1]).then_inc(h_hi, 1)
                for k in FIRST_HALVES[q]:
                    split(k)
            with loop(act, L, (U, HALVES), (T, TILES), (HD, HEADS), (N, SUMS), (G, DT), (FT, 2 * FF // P),
                      (FP, FF // P), (SQ, SQUARES), (STEP, ACT_STEPS), (W, SCALED), (X, 2 * DT)) as l:
                def four_tiles(after_split=None):
                    for pair in range(2):
                        split()
                        if after_split and pair == 0:
                            after_split()
                        take()
                        take()
                        U.up()

                halves(4)
                load_table(ACT.Sqrt)
                halves(2)
                act.wait_ge(scaled, W.at() + ONE_UP)
                four_tiles(lambda: root(D, rstd[:, :], p_st[:, 0:S + 2]))
                act.activation(suffix[:, :], cst[:, TRI:TRI + 2 * P], ACT.Copy)
                W.up(4)
                with loop(act, 3, (U, 8), (T, 4), (W, 4)):
                    halves(6)
                    four_tiles()
                    W.up(4)

                def token_tiles(dst, cg, n, factor):
                    halves(n)
                    for blk in range(2):
                        act.wait_ge(tiles_done, T.at(1))
                        act.activation(dst[:, blk, 512 * cg:512 * cg + S], res[T.const % BANKS][:, 0:S], ACT.Copy,
                                       scale=factor[:, blk:blk + 1]).then_inc(tmp_ready, 1)
                        T.up()

                act.wait_ge(h_ready, X.at(DT))
                act.wait_ge(par_in, 16)
                act.activation(norms[:, N2:BG], par[:, bass.ds(l * PCOLS + N2, BG - N2)], ACT.Copy).then_inc(gain_in, 1)
                act.wait_ge(rstd_ready, N.at() + ONE_UP)
                for cg in range(2):
                    token_tiles(v, cg, 8, rstd[:, S:S + 2])

                def c_tiles(first, n):
                    for k in range(first, first + n):
                        W.up()
                        act.wait_ge(scaled, W.at() + ONE_UP)
                        square(craw[:, k, :])
                        act.wait_ge(gain_in, l * 2 + 1)
                        hi_of = act.activation(chl[:, k, 0:S], craw[:, k, :], ACT.Copy, scale=norms[:, CG + k:CG + k + 1])
                    hi_of.then_inc(c_hi, 1)

                halves(6)
                four_tiles()
                split()
                c_tiles(0, 4)
                U.up()
                halves(2)
                split()
                root(CKV, rstd_kv[:, :], p_st[:, 0:S + 2])
                U.up()
                halves(2)
                four_tiles()
                split()
                c_tiles(CKVT, 4)
                U.up()
                halves(3)
                split()
                take()
                U.up()
                split()
                take()
                U.up()
                take(2)
                split()
                c_tiles(CKVT + 4, 2)
                W.up()
                take()
                take()
                U.up()
                for half in range(3):
                    split()
                    take()
                    take()
                    U.up()
                W.up(8)
                act.wait_ge(rstd_ready, N.at() + ONE_UP)
                token_tiles(mv, 0, 2, rstd_kv[:, S:S + 2])
                split()
                root(CQ, rstd_q[:, :], p_st[:, S:S + 2], MLA_SCALE)
                U.up()
                token_tiles(mv, 1, 1, rstd_kv[:, S:S + 2])
                at_tile = 0
                for u in range(10):
                    split()
                    U.up()
                    while at_tile < 12 and 6 * (at_tile + 1) <= 8 * (u + 1):
                        take()
                        at_tile += 1
                load_table(ACT.Exp)
                with loop(act, HEADS // 2, (U, 16), (T, 8), (HD, 2), (STEP, 4), (W, 8)) as i:
                    for e in range(2):
                        split()
                        U.up()
                        act.wait_ge(z_done, HD.at() + ONE_UP)
                        act.activation(k_st[:, :], flat(sbqk[:, bass.ds(i * 4 + 2 * e + 1, 1), :]), ACT.Copy,
                                       scale=SB_SCALE).then_inc(k_staged, 1)
                        split()
                        U.up()
                        split()
                        U.up()
                        act.wait_ge(scaled, W.at() + ONE_UP)
                        act.wait_ge(z_done, HD.at(1) + ONE_UP)
                        act.activation(sp[:, :], p_sb[:, 0:384], ACT.Abs).then_inc(act_step, 1)
                        act.wait_ge(act_step, STEP.at(1))
                        act.activation(sp[:, :], sp[:, :], ACT.Exp, scale=-1.0).then_inc(act_step, 1)
                        act.wait_ge(act_step, STEP.at(2))
                        STEP.up(2)
                        act.activation(sp[:, :], sp[:, :], ACT.Ln, bias=1.0).then_inc(ln_done, 1)
                        split()
                        U.up()
                        act.wait_ge(max_ready, HD.at(1))
                        act.activation(prob[:, 0:P], prob[:, 0:P], ACT.Exp, bias=stat[:, 2:3], accum_out=stat[:, 4:5])
                        act.activation(prob[:, P:384], prob[:, P:384], ACT.Exp, bias=stat[:, 3:4],
                                       accum_out=stat[:, 5:6]).then_inc(exp_done, 1)
                        act.wait_ge(sp_f32, HD.at(1))
                        act.activation(sp_hi[:, :], sp[:, :], ACT.Copy).then_inc(sp_hi_done, 1)
                        halves(2)
                        split()
                        act.wait_ge(logw_ready, HD.at(1))
                        act.activation(wgt[:, :], wgt[:, :], ACT.Exp).then_inc(w_ready, 1)
                        act.wait_ge(tr_done, HD.at(1))
                        act.activation(probT[:, :], p_tr[:, 0:384], ACT.Copy).then_inc(tr_copied, 1)
                        take()
                        take()
                        U.up()
                        split()
                        take()
                        take()
                        U.up()
                        act.wait_ge(osb_done, HD.at(1))
                        act.activation(flat(osb[:, bass.ds(i * 2 + e, 1), 0:S]), p_sb[:, 0:S], ACT.Copy).then_inc(osb_hi, 1)
                        act.wait_ge(om_done, HD.at(1) + ONE_UP)
                        act.activation(flat(omla[:, bass.ds(i * 2 + e, 1), 0:S]), p_ml[:, 0:S], ACT.Copy).then_inc(om_hi, 1)
                        HD.up()
                        W.up(4)
                def mixed(i, n):
                    for m in range(n, n + 2):
                        act.wait_ge(mix_f32, G.at(1))
                        act.activation(flat(blend[:, bass.ds(i * 4 + m, 1), 0:S]), pmla[:, m, :],
                                       ACT.Copy).then_inc(mix_hi, 1)
                        G.up()

                def sigmoids(i, n):
                    for m in range(n, n + 2):
                        for w in range(2):
                            sg = act.activation(sig[:, m, w * S:w * S + S], flat(gates[:, bass.ds(i * 8 + 2 * m + w, 1), :]),
                                                ACT.Sigmoid, bias=bias8[:, 2 * m + w:2 * m + w + 1])
                        sg.then_inc(sig_done, 1)

                def project(i, before):
                    split()
                    if before:
                        mixed(i - 1, 2)
                    U.up()
                    halves(1)
                    act.activation(bias8[:, :], par[:, bass.ds(l * PCOLS + i * 8 + BG, 8)], ACT.Copy).then_inc(act_step, 1)
                    STEP.up()
                    four_tiles()
                    split()
                    act.wait_ge(scaled, W.at() + ONE_UP)
                    act.wait_ge(act_step, STEP.at())
                    sigmoids(i, 0)
                    U.up()
                    split()
                    sigmoids(i, 2)
                    U.up()
                    split()
                    take()
                    take()
                    U.up()
                    split()
                    take()
                    take()
                    mixed(i, 0)
                    U.up()

                project(0, False)
                with loop(act, 3, (U, 8), (T, 8), (G, 4), (STEP, 1)) as i:
                    project(i + 1, True)

                def residual_tiles(i, next_norm, nhalves=6, gain=None, earlier=()):
                    def post(n):
                        for m in range(n, n + 2) if next_norm else ():
                            k = i * 4 + m
                            act.wait_ge(tiles_free, T.at(TILE_CREDIT - 1 + m - n))
                            square(flat(x[:, bass.ds(k, 1), :]))
                            g = gain4[:, m:m + 1] if gain is None else norms[:, gain + k:gain + k + 1]
                            act.activation(flat(h[:, bass.ds(k, 1), 0:S]), flat(x[:, bass.ds(k, 1), :]), ACT.Copy,
                                           scale=g).then_inc(h_hi, 1)
                            X.up()

                    for half in range(nhalves):
                        split()
                        if half < len(earlier):
                            earlier[half]()
                        U.up()
                    if next_norm and gain is None:
                        act.wait_ge(h_ready, X.at(DT))
                        act.activation(gain4[:, :], norms[:, bass.ds(i * 4 + N2, 4)], ACT.Copy).then_inc(act_step, 1)
                        STEP.up()
                    split()
                    take()
                    take()
                    U.up()
                    split()
                    if next_norm and gain is None:
                        act.wait_ge(act_step, STEP.at())
                    post(0)
                    take()
                    take()
                    U.up()
                    post(2)

                load_table(ACT.Sqrt)
                residual_tiles(0, True, earlier=[lambda: mixed(3, 2)])
                with loop(act, 3, (U, 8), (T, 4), (SQ, 4), (STEP, 1), (X, 4)) as i:
                    residual_tiles(i + 1, True)
                act.activation(norms[:, 0:DT], par[:, bass.ds(l * PCOLS + PCOLS, DT)], ACT.Copy).then_inc(gain_in, 1)

                def load_taps(dst, i, value, first):
                    act.wait_ge(conv_done, FT.at() + ONE_UP)
                    act.activation(dst[:, :], par[:, bass.ds(l * PCOLS + i * 32 + (CONV + 32 * first + 16 * value), 16)],
                                   ACT.Copy).then_inc(taps_in, 1)

                def tap2(m, dst, taps):
                    W.up()
                    act.wait_ge(scaled, W.at() + ONE_UP)
                    act.activation(dst[:, m, :], uconv[:, m, 2:2 + S], ACT.Identity, scale=taps[:, 4 * m + 2:4 * m + 3],
                                   bias=taps[:, 4 * m + 3:4 * m + 4]).then_inc(tap2_done, 1)
                    FT.up()

                def silu(m):
                    act.wait_ge(conv_done, FT.at(m - 3) + ONE_UP)
                    act.activation(fgate[:, m, :], fgate[:, m, :], ACT.Silu).then_inc(silu_done, 1)

                def product_hi(i, m):
                    act.wait_ge(ffn_f32, FP.at(1))
                    act.activation(flat(blend[:, bass.ds(i * 4 + m, 1), 0:S]), fgate[:, m, :], ACT.Copy).then_inc(ffn_hi, 1)
                    FP.up()

                def gate_group(i, first, part_start):
                    split()
                    if not part_start:
                        for m in range(2):
                            product_hi(i - 1, m)
                    U.up()
                    split()
                    if not part_start:
                        for m in range(2, 4):
                            product_hi(i - 1, m)
                    U.up()
                    halves(4)
                    load_taps(taps_g, i, 0, first)
                    split()
                    if part_start and first == 0:
                        act.wait_ge(scaled, W.at() + ONE_UP)
                        root(D, rstd[:, 0:S], p_st[:, 0:S])
                        load_table(ACT.Silu)
                    take()
                    take()
                    U.up()
                    split()
                    act.wait_ge(ffn_ready, FP.at(ACT_CREDIT))
                    act.wait_ge(taps_in, FT.at(4, 4, 1))
                    tap2(0, fgate, taps_g)
                    tap2(1, fgate, taps_g)
                    take()
                    take()
                    U.up()

                def value_group(i, first, last=False):
                    split()
                    tap2(2, fgate, taps_g)
                    tap2(3, fgate, taps_g)
                    U.up()
                    split()
                    for m in range(4):
                        silu(m)
                    U.up()
                    halves(4)
                    load_taps(taps_v, i, 1, first)
                    split()
                    take()
                    take()
                    U.up()
                    split()
                    act.wait_ge(taps_in, FT.at(4, 4, 1))
                    tap2(0, fval, taps_v)
                    tap2(1, fval, taps_v)
                    take()
                    take()
                    U.up()
                    if not last:
                        tap2(2, fval, taps_v)
                        tap2(3, fval, taps_v)

                def last_taps():
                    tap2(2, fval, taps_v)
                    tap2(3, fval, taps_v)

                def last_products(i):
                    for m in range(4):
                        product_hi(i, m)

                first = 0
                for groups in PARTS:
                    gate_group(0, first, True)
                    with loop(act, groups - 1, (U, 16), (T, 8), (FT, 8), (FP, 4), (W, 8)) as i:
                        value_group(i, first)
                        gate_group(i + 1, first, False)
                    value_group(groups - 1, first, last=True)
                    left = [last_taps, lambda: last_products(groups - 1)]
                    first += groups
                    if groups == 4:
                        residual_tiles(0, False, earlier=left)
                        with loop(act, 3, (U, 8), (T, 4)) as i:
                            residual_tiles(i + 1, False)
                    else:
                        act.wait_ge(gain_in, l * 2 + 2)
                        for i in range(4):
                            residual_tiles(i, True, 4, N1, left if i == 0 else ())
            act.wait_ge(scaled, W.at() + ONE_UP)
            load_table(ACT.Sqrt)
            root(D, rstd[:, 0:S], p_st[:, 0:S])
            act.wait_ge(h_ready, X.at(DT))
            for k in range(DT - 4, DT):
                y = act.activation(x[:, k, :], x[:, k, :], ACT.Copy, scale=norms[:, N1 + k:N1 + k + 1])
            y.then_inc(y_gained, 1)

        @block.vector
        def _(dve):
            U, T, HD, N, G, FT, FP, STEP, X = (Count() for _ in range(9))
            dve.sem_inc(tiles_free, TILE_CREDIT)
            dve.sem_inc(ffn_ready, ACT_CREDIT)
            for started in (osb_free, om_free, conv_done, rstd_ready):
                dve.sem_inc(started, ONE_UP)

            def flat(t):
                return t.rearrange("p a t -> p (a t)")

            def step(ins):
                ins.then_inc(dve_step, 1)
                STEP.up()
                dve.wait_ge(dve_step, STEP.at())

            def split(k=AHEAD):
                u = U.const + k
                part = slice(8 * (u % 2), 8 * (u % 2) + 8)
                dve.wait_ge(hi_done, U.at(k + 1))
                dve.tensor_tensor(lo[:, u // 2 % RAW, part, :], raw[:, u // 2 % RAW, part, :],
                                  hi[:, u % HIS, :, :].bitcast(F32), ALU.subtract).then_inc(split_done, 1)

            def halves(n):
                for _ in range(n):
                    split()
                    U.up()

            def join(dst, last=1):
                dve.wait_ge(tmp_ready, T.at(1))
                dve.tensor_tensor(dst, res[T.const % BANKS][:, 0:S], tmp[:, T.const % 2, :], ALU.add).then_inc(tiles_free, last)
                T.up(last)

            def make_rstd(dst):
                dve.wait_ge(root_ready, N.at(1))
                dve.reciprocal(dst, dst).then_inc(rstd_ready, 1)
                N.up()

            def low_h(k, gain):
                dve.wait_ge(h_hi, X.at(1))
                dve.scalar_tensor_tensor(out=flat(h[:, bass.ds(k, 1), S:2 * S]), in0=flat(x[:, bass.ds(k, 1), :]),
                                         scalar=gain, in1=flat(h[:, bass.ds(k, 1), 0:S].bitcast(F32)),
                                         op0=ALU.mult, op1=ALU.subtract).then_inc(h_ready, 1)
                X.up()

            dve.wait_ge(gain1_in, 16)
            for q in range(4):
                for k in range(4 * q, 4 * q + 4):
                    low_h(k, par[:, N1 + k:N1 + k + 1])
                for k in FIRST_HALVES[q]:
                    split(k)
            with loop(dve, L, (U, HALVES), (T, TILES), (HD, HEADS), (N, SUMS), (G, DT), (FT, 2 * FF // P),
                      (FP, FF // P), (STEP, DVE_STEPS), (X, 2 * DT)) as l:
                def four_tiles(dst, after_split=None):
                    for pair in range(2):
                        split()
                        if after_split and pair == 0:
                            after_split()
                        for m in range(2):
                            join(dst(2 * pair + m))
                        U.up()

                def qk(i, after_split=None):
                    halves(6)
                    four_tiles(lambda m: flat(sbqk[:, bass.ds(i * 4 + m, 1), :]), after_split)

                qk(0, lambda: make_rstd(rstd[:, :]))
                with loop(dve, 3, (U, 8), (T, 4)) as i:
                    qk(i + 1)

                def token_tiles(dst, cg, n, factor):
                    halves(n)
                    for blk in range(2):
                        dve.wait_ge(tmp_ready, T.at(1))
                        dve.tensor_scalar(dst[:, blk, 512 * cg + S:512 * cg + 2 * S], res[T.const % BANKS][:, S:2 * S],
                                          factor[:, blk:blk + 1], None, ALU.mult).then_inc(tiles_free, 1)
                        T.up()

                def low_c(first, n, number):
                    dve.wait_ge(c_hi, number)
                    for k in range(first, first + n):
                        ins = dve.scalar_tensor_tensor(out=chl[:, k, S:2 * S], in0=craw[:, k, :],
                                                       scalar=norms[:, CG + k:CG + k + 1],
                                                       in1=chl[:, k, 0:S].bitcast(F32), op0=ALU.mult, op1=ALU.subtract)
                    ins.then_inc(c_ready, 1)

                for cg in range(2):
                    token_tiles(v, cg, 8, rstd[:, S:S + 2])
                halves(6)
                four_tiles(lambda m: craw[:, m, :])
                halves(2)
                low_c(0, 4, l * 3 + 1)
                halves(2)
                split()
                make_rstd(rstd_kv[:, :])
                U.up()
                halves(1)
                four_tiles(lambda m: craw[:, CKVT + m, :])
                halves(2)
                low_c(CKVT, 4, l * 3 + 2)
                halves(2)
                split()
                join(craw[:, CKVT + 4, :])
                U.up()
                split()
                join(craw[:, CKVT + 5, :])
                U.up()
                join(kr[:, :], 2)
                four_tiles(lambda m: mqk[:, 2 * m + 1, :])
                low_c(CKVT + 4, 2, l * 3 + 3)
                four_tiles(lambda m: mqk[:, 2 * (4 + m) + 1, :])
                token_tiles(mv, 0, 2, rstd_kv[:, S:S + 2])
                split()
                make_rstd(rstd_q[:, :])
                U.up()
                token_tiles(mv, 1, 1, rstd_kv[:, S:S + 2])
                at_tile = 0
                for u in range(10):
                    split()
                    U.up()
                    while at_tile < 12 and 6 * (at_tile + 1) <= 8 * (u + 1):
                        join(qr[:, at_tile, :] if at_tile < 4 else mqk[:, 2 * (at_tile - 4), :])
                        at_tile += 1
                with loop(dve, HEADS // 2, (U, 16), (T, 8), (HD, 2), (STEP, 2 * DVE_HEAD_STEPS)) as i:
                    for e in range(2):
                        def gate_tile(m):
                            join(flat(gates[:, bass.ds(i * 8 + 4 * e + m, 1), :]))

                        halves(3)
                        dve.wait_ge(s_done, HD.at(1))
                        dve.scalar_tensor_tensor(out=prob[:, 0:P], in0=p_ml[:, 0:P], scalar=rstd_q[:, 0:1],
                                                 in1=c_(MNEG), op0=ALU.mult, op1=ALU.add)
                        step(dve.scalar_tensor_tensor(out=prob[:, P:384], in0=p_ml[:, P:384], scalar=rstd_q[:, 1:2],
                                                      in1=c_(MNEG + P, S), op0=ALU.mult, op1=ALU.add))
                        dve.tensor_reduce(stat[:, 0:1], prob[:, 0:P], AX.X, ALU.max)
                        step(dve.tensor_reduce(stat[:, 1:2], prob[:, P:384], AX.X, ALU.max))
                        dve.tensor_scalar(stat[:, 2:4], stat[:, 0:2], -1.0, None, ALU.mult).then_inc(max_ready, 1)
                        halves(1)
                        dve.wait_ge(ln_done, HD.at(1))
                        step(dve.scalar_tensor_tensor(out=sp[:, :], in0=p_sb[:, 0:384], scalar=0.0, in1=sp[:, :],
                                                      op0=ALU.max, op1=ALU.add))
                        diagonal = sp[:, :].rearrange("p (b t) -> p b t", b=3)[:, 0:3:2, :]
                        keep = c_(KEEP, S).rearrange("p (b t) -> p b t", b=2)
                        dve.tensor_tensor(diagonal, diagonal, keep, ALU.mult).then_inc(sp_f32, 1)
                        halves(1)
                        dve.wait_ge(sp_hi_done, HD.at(1))
                        dve.tensor_tensor(sp_lo[:, :], sp[:, :], sp_hi[:, :].bitcast(F32), ALU.subtract).then_inc(sp_ready, 1)
                        dve.wait_ge(exp_done, HD.at(1))
                        step(dve.reciprocal(stat[:, 4:6], stat[:, 4:6]))
                        dve.tensor_scalar(prob[:, 0:P], prob[:, 0:P], stat[:, 4:5], None, ALU.mult)
                        dve.tensor_scalar(prob[:, P:384], prob[:, P:384], stat[:, 5:6], None, ALU.mult).then_inc(prob_ready, 1)
                        halves(1)
                        split()
                        dve.wait_ge(p_done, HD.at(1))
                        dve.scalar_tensor_tensor(out=wgt[:, :], in0=p_sb[:, 0:384], scalar=0.0, in1=c_(SBNEG, 384),
                                                 op0=ALU.min, op1=ALU.add).then_inc(logw_ready, 1)
                        gate_tile(0)
                        gate_tile(1)
                        U.up()
                        split()
                        gate_tile(2)
                        gate_tile(3)
                        U.up()
                        for out, o_hi, done, free in ((osb, osb_hi, p_sb, osb_free), (omla, om_hi, p_ml, om_free)):
                            dve.wait_ge(o_hi, HD.at(1))
                            o = out[:, bass.ds(i * 2 + e, 1), :]
                            dve.tensor_tensor(flat(o[:, :, S:2 * S]), done[:, 0:S], flat(o[:, :, 0:S].bitcast(F32)),
                                              ALU.subtract).then_inc(free, 1)
                        HD.up()
                def mix(n):
                    dve.wait_ge(sig_done, G.at(2))
                    dve.wait_ge(tiles_free, T.at(TILE_CREDIT))
                    dve.tensor_tensor(pmla[:, n, :], pmla[:, n, :], sig[:, n, S:2 * S], ALU.mult)
                    step(dve.tensor_tensor(pmla[:, n + 1, :], pmla[:, n + 1, :], sig[:, n + 1, S:2 * S], ALU.mult))
                    dve.wait_ge(psb_gated, G.at(2))
                    for m in range(n, n + 2):
                        dve.tensor_tensor(pmla[:, m, :], pmla[:, m, :], psb[:, m, :], ALU.add).then_inc(mix_f32, 1)

                def mix_lo(i, n):
                    for m in range(n, n + 2):
                        dve.wait_ge(mix_hi, G.at(1))
                        b = blend[:, bass.ds(i * 4 + m, 1), :]
                        dve.tensor_tensor(flat(b[:, :, S:2 * S]), pmla[:, m, :],
                                          flat(b[:, :, 0:S].bitcast(F32)), ALU.subtract).then_inc(mix_ready, 1)
                        G.up()

                def project(i, before):
                    split()
                    if before:
                        mix(2)
                    U.up()
                    split()
                    if before:
                        mix_lo(i - 1, 2)
                    U.up()
                    for pair in range(2):
                        join(psb[:, 2 * pair, :])
                        join(psb[:, 2 * pair + 1, :])
                        split()
                        U.up()
                    halves(2)
                    split()
                    if before:
                        dve.wait_ge(mix_ready, G.at())
                    join(pmla[:, 0, :])
                    join(pmla[:, 1, :])
                    U.up()
                    split()
                    mix(0)
                    join(pmla[:, 2, :])
                    join(pmla[:, 3, :])
                    mix_lo(i, 0)
                    U.up()

                project(0, False)
                with loop(dve, 3, (U, 8), (T, 8), (G, 4), (STEP, 2)) as i:
                    project(i + 1, True)

                def residual_tiles(i, next_norm, nhalves=6, gain=None, earlier=()):
                    def pair(n):
                        xs = [flat(x[:, bass.ds(i * 4 + n + e, 1), :]) for e in range(2)]
                        for e in range(2):
                            dve.wait_ge(tmp_ready, T.at(1 + e))
                            added = dve.tensor_tensor(xs[e], xs[e], tmp[:, (T.const + e) % 2, :], ALU.add)
                        step(added)
                        for e in range(2):
                            dve.tensor_tensor(xs[e], res[T.const % BANKS][:, 0:S], xs[e], ALU.add).then_inc(tiles_free, 1)
                            T.up()

                    def low(n):
                        for m in range(n, n + 2) if next_norm else ():
                            low_h(i * 4 + m, gain4[:, m:m + 1] if gain is None else norms[:, gain + 4 * i + m:gain + 4 * i + m + 1])

                    for half in range(nhalves):
                        split()
                        if half < len(earlier):
                            earlier[half]()
                        U.up()
                    split()
                    pair(0)
                    U.up()
                    split()
                    low(0)
                    pair(2)
                    U.up()
                    low(2)

                residual_tiles(0, True, earlier=[lambda: mix(2), lambda: mix_lo(3, 2)])
                with loop(dve, 3, (U, 8), (T, 4), (STEP, 2), (X, 4)) as i:
                    residual_tiles(i + 1, True)
                step(dve.memset(uconv[:, :, 0:2], 0.0))

                def convs(n, dst, taps):
                    def tap(m, back):
                        return dve.scalar_tensor_tensor(out=dst[:, m, :], in0=uconv[:, m, 2 - back:2 - back + S],
                                                        scalar=taps[:, 4 * m + 2 - back:4 * m + 3 - back],
                                                        in1=dst[:, m, :], op0=ALU.mult, op1=ALU.add)

                    dve.wait_ge(tap2_done, FT.at(1))
                    tap(n, 1)
                    dve.wait_ge(tap2_done, FT.at(2))
                    step(tap(n + 1, 1))
                    for m in range(n, n + 2):
                        tap(m, 2).then_inc(conv_done, 1)
                    FT.up(2)

                def product_lo(i, m):
                    dve.wait_ge(ffn_hi, FP.at(1))
                    b = blend[:, bass.ds(i * 4 + m, 1), :]
                    dve.tensor_tensor(flat(b[:, :, S:2 * S]), fgate[:, m, :], flat(b[:, :, 0:S].bitcast(F32)),
                                      ALU.subtract).then_inc(ffn_ready, 1)
                    FP.up()

                def group_tiles(dst, taps, after_split=None):
                    split()
                    if after_split:
                        after_split()
                    join(uconv[:, 0, 2:2 + S])
                    join(uconv[:, 1, 2:2 + S])
                    U.up()
                    split()
                    convs(0, dst, taps)
                    join(uconv[:, 2, 2:2 + S])
                    join(uconv[:, 3, 2:2 + S])
                    U.up()

                def gate_group(i, part_start, after_split=None):
                    if part_start:
                        halves(6)
                    else:
                        split()
                        product_lo(i - 1, 0)
                        product_lo(i - 1, 1)
                        U.up()
                        split()
                        product_lo(i - 1, 2)
                        product_lo(i - 1, 3)
                        U.up()
                        halves(4)
                    group_tiles(fgate, taps_g, after_split)

                def value_group(last=False):
                    split()
                    convs(2, fgate, taps_g)
                    U.up()
                    halves(5)
                    group_tiles(fval, taps_v)
                    if not last:
                        convs(2, fval, taps_v)

                def last_convs():
                    convs(2, fval, taps_v)

                def last_products(i, n):
                    for m in range(n, n + 2):
                        product_lo(i, m)

                def second_rstd():
                    make_rstd(rstd[:, 0:S])

                for part, groups in enumerate(PARTS):
                    gate_group(0, True, second_rstd if part == 0 else None)
                    with loop(dve, groups - 1, (U, 16), (T, 8), (FT, 8), (FP, 4), (STEP, 4)) as i:
                        value_group()
                        gate_group(i + 1, False)
                    value_group(last=True)
                    left = [last_convs, lambda: last_products(groups - 1, 0), lambda: last_products(groups - 1, 2)]
                    if groups == 4:
                        residual_tiles(0, False, earlier=left)
                        with loop(dve, 3, (U, 8), (T, 4), (STEP, 2)) as i:
                            residual_tiles(i + 1, False)
                    else:
                        for i in range(4):
                            residual_tiles(i, True, 4, N1, left if i == 0 else ())
            make_rstd(rstd[:, 0:S])
            dve.wait_ge(rstd_ready, N.at() + ONE_UP)
            for q in range(3):
                for k in range(4 * q, 4 * q + 4):
                    ins = dve.scalar_tensor_tensor(out=x[:, k, :], in0=x[:, k, :],
                                                   scalar=par[:, L * PCOLS + k:L * PCOLS + k + 1], in1=rstd[:, 0:S],
                                                   op0=ALU.mult, op1=ALU.mult)
                ins.then_inc(x_done, 1)

        @block.gpsimd
        def _(pool):
            SQ, N, HD, G, STEP, T, W, FP = (Count() for _ in range(8))
            pool.sem_inc(scaled, ONE_UP)

            def flat(t):
                return t.rearrange("p a t -> p (a t)")

            def step(ins):
                ins.then_inc(pool_step, 1)
                STEP.up()
                pool.wait_ge(pool_step, STEP.at())

            def scale(t, factor, last=1):
                pool.wait_ge(tiles_free, T.at(1 + TILE_CREDIT))
                pool.tensor_tensor(t, t, factor[:, 0:S], ALU.mult).then_inc(scaled, 1)
                T.up(last)
                W.up()

            def add_squares(n, fresh=True):
                if fresh:
                    pool.wait_ge(sum_done, N.at() + ONE_UP)
                    N.up()
                    pool.wait_ge(sq_ready, SQ.at(2))
                    pool.tensor_tensor(sqsum[:, :], sq[:, 0, :], sq[:, 1, :], ALU.add).then_inc(sq_added, 2)
                    SQ.up(2)
                    n -= 2
                for _ in range(n):
                    pool.wait_ge(sq_ready, SQ.at(1))
                    pool.wait_ge(sq_added, SQ.at())
                    pool.tensor_tensor(sqsum[:, :], sqsum[:, :], sq[:, SQ.const % 2, :], ALU.add).then_inc(sq_added, 1)
                    SQ.up()

            def rotate(t):
                for q in range(0, P, 32):
                    o = q ^ 32
                    step(pool.tensor_tensor(swap[q:q + 32, :], t[o:o + 32, :], cst[o:o + 32, SIN:SIN + S], ALU.mult))
                step(pool.tensor_tensor(t, t, c_(COS, S), ALU.mult))
                pool.tensor_tensor(t, t, swap[:, :], ALU.add).then_inc(rope_done, 1)

            for q in range(4):
                quad = xsq[:, 4 * q:4 * q + 4, :]
                pool.wait_ge(x_landed[q], 16)
                step(pool.tensor_tensor(quad, x[:, 4 * q:4 * q + 4, :], x[:, 4 * q:4 * q + 4, :], ALU.mult))
                if q:
                    step(pool.tensor_tensor(xsq[:, 0:4, :], xsq[:, 0:4, :], quad, ALU.add))
            step(pool.tensor_tensor(xsq[:, 0:2, :], xsq[:, 0:2, :], xsq[:, 2:4, :], ALU.add))
            pool.tensor_tensor(sqsum[:, :], xsq[:, 0, :], xsq[:, 1, :], ALU.add).then_inc(sq_added, DT)
            SQ.up(DT)
            N.up()
            with loop(pool, L, (SQ, SQUARES), (N, SUMS), (HD, HEADS), (G, DT), (STEP, POOL_STEPS), (T, TILES),
                      (W, SCALED), (FP, FF // P)) as l:
                pool.wait_ge(rstd_ready, N.at() + ONE_UP)
                for m in range(4):
                    scale(sbqk[:, m, :], rstd)
                with loop(pool, 3, (T, 4), (W, 4)) as i:
                    for m in range(4):
                        scale(flat(sbqk[:, bass.ds(i * 4 + (4 + m), 1), :]), rstd)
                T.up(4)
                for k in range(CKVT):
                    scale(craw[:, k, :], rstd)
                add_squares(4)
                for k in range(4):
                    scale(craw[:, CKVT + k, :], rstd)
                add_squares(4)
                for k in range(2):
                    scale(craw[:, CKVT + 4 + k, :], rstd)
                scale(kr[:, :], rstd, 2)
                add_squares(2, fresh=False)
                pool.wait_ge(scaled, W.at() + ONE_UP)
                pool.wait_ge(sq_added, SQ.at())
                rotate(kr[:, :])
                pool.wait_ge(rstd_ready, N.at(-1) + ONE_UP)
                for m in range(HEADS):
                    scale(mqk[:, 2 * m + 1, :], rstd_kv)
                T.up(4)
                pool.wait_ge(rope_done, l * 5 + 1)
                pool.wait_ge(scaled, W.at() + ONE_UP)
                for p in range(HEADS // 2):
                    T.up()
                    pool.wait_ge(tiles_free, T.at(TILE_CREDIT))
                    rotate(qr[:, p, :])
                    if p < HEADS // 2 - 1:
                        pool.wait_ge(rope_done, l * 5 + (p + 2))
                T.up(HEADS)
                with loop(pool, HEADS // 2, (HD, 2), (T, 8), (W, 8)) as i:
                    for e in range(2):
                        def head_cols(t, b):
                            return t[:, b, bass.ds(i * (2 * P) + e * P, P)]

                        pool.wait_ge(om_done, HD.at() + ONE_UP)
                        pool.wait_ge(rope_done, l * 5 + 5)
                        pool.wait_ge(tiles_free, T.at(TILE_CREDIT))
                        pool.tensor_copy(qn_st[:, :], flat(mqk[:, bass.ds(i * 4 + 2 * e, 1), :]))
                        if e == 0:
                            pool.tensor_copy(qr_st[:, :], flat(qr[:, bass.ds(i, 1), :]))
                        for b in range(2):
                            pool.tensor_copy(v_st[:, b, :], head_cols(v, b))
                            ins = pool.tensor_copy(mv_st[:, b, :], head_cols(mv, b))
                        ins.then_inc(staged, 1)
                        HD.up()
                        for m in range(4):
                            scale(flat(gates[:, bass.ds(i * 8 + (4 * e + m), 1), :]), rstd)
                with loop(pool, 4, (G, 4), (T, 8)):
                    for m in range(4):
                        pool.wait_ge(sig_done, G.at(1))
                        pool.wait_ge(tiles_free, T.at(m + 1 + TILE_CREDIT))
                        pool.tensor_tensor(psb[:, m, :], psb[:, m, :], sig[:, m, 0:S], ALU.mult).then_inc(psb_gated, 1)
                        G.up()
                    T.up(8)
                T.up(DT)
                add_squares(DT)
                pool.wait_ge(rstd_ready, N.at() + ONE_UP)

                def group():
                    for m in range(4):
                        scale(uconv[:, m, 2:2 + S], rstd)

                def products():
                    for m in range(4):
                        pool.wait_ge(silu_done, FP.at(1))
                        pool.wait_ge(conv_done, FP.at(0, 4, 8, 4 + m + 1 + ONE_UP))
                        pool.tensor_tensor(fgate[:, m, :], fgate[:, m, :], fval[:, m, :], ALU.mult).then_inc(ffn_f32, 1)
                        FP.up()

                for groups in PARTS:
                    group()
                    with loop(pool, groups - 1, (T, 8), (W, 8), (FP, 4)):
                        group()
                        products()
                        group()
                    group()
                    products()
                    T.up(DT)
                add_squares(DT)
            pool.wait_ge(y_gained, 1)
            pool.wait_ge(rstd_ready, N.at() + ONE_UP)
            for k in range(DT - 4, DT):
                y = pool.tensor_tensor(x[:, k, :], x[:, k, :], rstd[:, 0:S], ALU.mult)
            y.then_inc(y_done, 1)


ACT_STEPS = 2 * HEADS + 4 + 4
DVE_HEAD_STEPS = 4
DVE_STEPS = HEADS * DVE_HEAD_STEPS + DT // 2 + DT // 2 + 1 + FF // P + 3 * DT // 2
POOL_STEPS = 5 * 5


def _tiles(w):
    k, m = w.shape
    return w.reshape(k // P, P, m // P, P).transpose(0, 2, 1, 3)


def _blocked(w, kb=4, nm=4):
    t = _tiles(w)
    out = []
    for m0 in range(0, t.shape[1], nm):
        for k0 in range(0, t.shape[0], kb):
            out.append(t[k0:k0 + kb, m0:m0 + nm].transpose(1, 0, 2, 3).reshape(-1, P, P))
    return np.concatenate(out)


def _rows(w):
    t = _tiles(w)
    return np.concatenate([t[:, m:m + 4].reshape(-1, P, P) for m in range(0, t.shape[1], 4)])


def _layer_stream(w_in, w_uq, w_ukv, w_psb, w_pmla, w_out, w_up, w_down):
    cut = np.cumsum([0, 1024, 1024, 1024, CQ, CKV, ROPE, D, D])
    q, k, v, cq, ckv, kr, gs, gm = (w_in[:, a:b] for a, b in zip(cut[:-1], cut[1:]))
    pair = lambda a, b: np.stack([a.reshape(len(a), -1, P), b.reshape(len(b), -1, P)], 2).reshape(len(a), -1)
    uq = w_uq.reshape(CQ, HEADS, P + ROPE)
    ukv = w_ukv.reshape(CKV, HEADS, 2, P)
    parts = [
        _blocked(pair(q, k)), _rows(v), _blocked(ckv), _blocked(cq[:, :512]),
        _blocked(np.concatenate([cq[:, 512:], kr, kr], 1), 4, 3),
        _blocked(ukv[:, :, 0].reshape(CKV, -1)), _rows(ukv[:, :, 1].reshape(CKV, -1)),
        _blocked(uq[:, :, P:].reshape(CQ, -1), CQT, 4), _blocked(uq[:, :, :P].reshape(CQ, -1), CQT, 8),
        np.zeros((8, P, P), w_in.dtype),
        _blocked(pair(gs, gm)),
    ]
    a, b = _blocked(w_psb), _blocked(w_pmla)
    for g in range(4):
        parts += [a[32 * g:32 * g + 32], b[32 * g:32 * g + 32]]
    parts.append(_blocked(w_out))
    g0 = 0
    for n in PARTS:
        for g in range(g0, g0 + n):
            parts += [_blocked(w_up[:, 512 * g:512 * g + 512]), _blocked(w_up[:, FF + 512 * g:FF + 512 * g + 512])]
        parts.append(_blocked(w_down[512 * g0:512 * (g0 + n)]))
        g0 += n
    t = np.concatenate(parts)
    assert len(t) == 8 * HALVES, len(t)
    return t.reshape(HALVES // 2, 16, P, P).transpose(0, 2, 1, 3)


def _consts():
    c = np.zeros((P, CCOLS), np.float32)
    inv = 1.0 / (np.float32(10000.0) ** (np.arange(0, ROPE, 2, dtype=np.float32) / np.float32(ROPE)))
    ang = np.arange(S, dtype=np.float32)[:, None] * inv[None, :].astype(np.float32)
    c[:, COS:COS + S] = np.tile(np.cos(ang).T, (4, 1))
    c[:, SIN:SIN + S] = np.tile(np.concatenate([np.sin(ang).T, -np.sin(ang).T]), (2, 1))
    p, f = np.arange(P)[:, None], np.arange(P)[None, :]
    keep = (p < f).astype(np.float32)
    seen = f // 64 <= p // 64
    c[:, KEEP:KEEP + 2 * P] = np.tile(keep, 2)
    for b in (0, 2):
        c[:, SBNEG + b * P:SBNEG + b * P + P] = np.where(keep > 0, 0, MASKED)
        c[:, MNEG + b * P:MNEG + b * P + P] = np.where(seen, 0, MASKED)
    c[:, TRI:TRI + P] = np.where(p >= f, -1, 0)
    c[:, NEG:NEG + P] = -1
    c[:, ONE:ONE + P] = 1
    c[:, EYE:EYE + P] = np.eye(P)
    return c


def kernel(x, norm1_g, w_in, b_gate, q_norm_g, w_uq, kv_norm_g, w_ukv, w_proj_sb, w_proj_mla, w_out,
           norm2_g, w_up, conv_w, conv_b, w_down, final_g):
    import concourse.bacc as bacc
    from concourse.bass_utils import run_bass_kernel_spmd

    a = [np.asarray(t) for t in (w_in, w_uq, w_ukv, w_proj_sb, w_proj_mla, w_out, w_up, w_down)]
    stream = np.zeros((CHUNKS + 2, P, 16, P), a[0].dtype)
    for l in range(L):
        stream[l * HALVES // 2:(l + 1) * HALVES // 2] = _layer_stream(*(t[l] for t in a))

    def cols(t):
        return np.asarray(t).reshape(-1, P).T

    par = []
    for l in range(L):
        bg = np.asarray(b_gate[l]).reshape(2, DT, P).transpose(2, 1, 0).reshape(P, 2 * DT)
        taps = np.concatenate([np.asarray(conv_w[l]), np.asarray(conv_b[l])[None]])
        taps = taps.reshape(4, 2, sum(PARTS), 4, P).transpose(4, 2, 1, 3, 0).reshape(P, -1)
        par += [cols(norm1_g[l]), cols(norm2_g[l]), cols(kv_norm_g[l]), cols(q_norm_g[l]), bg, taps]
    par = np.ascontiguousarray(np.concatenate(par + [cols(final_g)], 1))
    xt = np.ascontiguousarray(np.asarray(x)[0].T.reshape(DT, P, S).transpose(1, 0, 2))

    nc = bacc.Bacc("TRN2", target_bir_lowering=False, num_devices=1)
    ins = {"x_t": xt, "stream": stream, "par_in": par, "cst_in": _consts()}
    args = [nc.dram_tensor(n, t.shape, F32, kind="ExternalInput").ap() for n, t in ins.items()]
    y = nc.dram_tensor("y_t", (P, DT, S), F32, kind="ExternalOutput").ap()
    trunk(nc, *args, y)
    r = run_bass_kernel_spmd(nc, [ins], core_ids=[0])
    got = r.results[0]["y_t"]
    return np.ascontiguousarray(got.transpose(1, 0, 2).reshape(D, S).T[None])
```
